# Optimizing a Trainium2 kernel written in Bass

```python
import math
import jax, jax.numpy as jnp
from jax import lax
import numpy as np

D_MODEL = 1024
BATCH = 1
SEQ = 512
DEPTH = 1

CONV_WIDTH = 1024
CONV_K = 3
MLSTM_HEADS = 8
MLSTM_DQK = 128
MLSTM_DV = 128
MLSTM_CHUNK = 64
MLSTM_QK_W = MLSTM_HEADS * MLSTM_DQK
MLSTM_V_W = MLSTM_HEADS * MLSTM_DV
RMS_EPS = 1e-6
N_BRANCHES = 2
N_EXPERTS = 64
N_GROUPS = 8
TOPK_GROUPS = 4
GROUP_SCORE_TOPK = 2
TOP_K = 8
D_EXPERT = 256
D_SHARED = 256
ROUTED_SCALE = 2.5
PLE_DIM = 256
ALPHA = (2 * DEPTH) ** 0.25
BETA = (8 * DEPTH) ** -0.25
LN_EPS = 1e-5
IN_WIDTH = 3 * CONV_WIDTH + 2 * MLSTM_QK_W + 2 * MLSTM_V_W + 2 * MLSTM_HEADS + N_BRANCHES * D_MODEL

kernel_name = 'hybrid_conv_mlstm_moe_deepnorm'

def layer_norm(x, g, b):
    xf = x.astype(jnp.float32)
    mu = xf.mean(-1, keepdims=True)
    var = jnp.square(xf - mu).mean(-1, keepdims=True)
    return ((xf - mu) * lax.rsqrt(var + LN_EPS) * g + b).astype(x.dtype)

def split_columns(z):
    sizes = (CONV_WIDTH, CONV_WIDTH, CONV_WIDTH, MLSTM_QK_W, MLSTM_QK_W, MLSTM_V_W,
             MLSTM_V_W, MLSTM_HEADS, MLSTM_HEADS, N_BRANCHES * D_MODEL)
    offsets = []
    acc = 0
    for s in sizes[:-1]:
        acc += s
        offsets.append(acc)
    return jnp.split(z, offsets, axis=-1)

def short_conv_branch(gate_in, gate_out, val, conv_w):
    u = gate_in * val
    seq = u.shape[1]
    u_pad = jnp.pad(u, ((0, 0), (CONV_K - 1, 0), (0, 0)))
    conv = sum(conv_w[j] * u_pad[:, j:j + seq] for j in range(CONV_K))
    return gate_out * conv

def mlstm_branch(q, k, v, o, i_pre, f_pre, norm_g):
    f32 = jnp.float32
    bsz, seq, _ = q.shape
    nc = seq // MLSTM_CHUNK
    L = MLSTM_CHUNK

    def heads(t, d):
        return t.astype(f32).reshape(bsz, nc, L, MLSTM_HEADS, d).transpose(0, 3, 1, 2, 4)

    def gates(t):
        return t.astype(f32).reshape(bsz, nc, L, MLSTM_HEADS).transpose(0, 3, 1, 2)

    qh = heads(q, MLSTM_DQK) * (MLSTM_DQK ** -0.5)
    kh = heads(k, MLSTM_DQK)
    vh = heads(v, MLSTM_DV)
    ig = gates(i_pre)
    log_f = jax.nn.log_sigmoid(gates(f_pre))
    b = jnp.cumsum(log_f, axis=-1)
    b_last = b[..., -1]

    a = b_last[..., None] - b + ig
    m_loc = jnp.max(a, axis=-1)
    w_loc = jnp.exp(a - m_loc[..., None])
    c_loc = jnp.einsum('bhcsk,bhcsv->bhckv', kh * w_loc[..., None], vh)
    n_loc = jnp.einsum('bhcs,bhcsk->bhck', w_loc, kh)

    def step(carry, inp):
        c, n, m = carry
        bl, ml, cl, nl = inp
        m_new = jnp.maximum(bl + m, ml)
        sp = jnp.exp(bl + m - m_new)
        sl = jnp.exp(ml - m_new)
        c_new = sp[..., None, None] * c + sl[..., None, None] * cl
        n_new = sp[..., None] * n + sl[..., None] * nl
        return (c_new, n_new, m_new), (c, n, m)

    init = (jnp.zeros((bsz, MLSTM_HEADS, MLSTM_DQK, MLSTM_DV), f32),
            jnp.zeros((bsz, MLSTM_HEADS, MLSTM_DQK), f32),
            jnp.zeros((bsz, MLSTM_HEADS), f32))
    xs = (jnp.moveaxis(b_last, 2, 0), jnp.moveaxis(m_loc, 2, 0),
          jnp.moveaxis(c_loc, 2, 0), jnp.moveaxis(n_loc, 2, 0))
    _, (c_prev, n_prev, m_prev) = lax.scan(step, init, xs)
    c_prev = jnp.moveaxis(c_prev, 0, 2)
    n_prev = jnp.moveaxis(n_prev, 0, 2)
    m_prev = jnp.moveaxis(m_prev, 0, 2)

    log_inter = b + m_prev[..., None]
    causal = jnp.tril(jnp.ones((L, L), dtype=bool))
    log_d = jnp.where(causal, b[..., :, None] - b[..., None, :] + ig[..., None, :], -jnp.inf)
    m_out = jnp.maximum(log_inter, jnp.max(log_d, axis=-1))
    d = jnp.exp(log_d - m_out[..., None])
    s = jnp.einsum('bhcjk,bhcsk->bhcjs', qh, kh) * d
    w_inter = jnp.exp(log_inter - m_out)
    num = (jnp.einsum('bhcjs,bhcsv->bhcjv', s, vh)
           + w_inter[..., None] * jnp.einsum('bhcjk,bhckv->bhcjv', qh, c_prev))
    den = s.sum(-1) + w_inter * jnp.einsum('bhcjk,bhck->bhcj', qh, n_prev)
    h = num / jnp.maximum(jnp.abs(den), jnp.exp(-m_out))[..., None]

    h = h.transpose(0, 2, 3, 1, 4).reshape(bsz, seq, MLSTM_HEADS, MLSTM_DV)
    h = h * lax.rsqrt(jnp.mean(jnp.square(h), axis=-1, keepdims=True) + RMS_EPS)
    h = h.reshape(bsz, seq, MLSTM_V_W) * norm_g
    return (h * jax.nn.sigmoid(o.astype(f32))).astype(q.dtype)

def hybrid_mixer(x, w_in, conv_w, b_igate, b_fgate, norm_g, w_branch_a, w_branch_b, w_out):
    z = x @ w_in
    c_in, c_out, c_val, q, k, v, o, ig, fg, merge = split_columns(z)
    y_a = short_conv_branch(c_in, c_out, c_val, conv_w)
    y_b = mlstm_branch(q, k, v, o, ig + b_igate, fg + b_fgate, norm_g)
    g = jax.nn.sigmoid(merge).reshape(merge.shape[:-1] + (N_BRANCHES, D_MODEL))
    mixed = g[..., 0, :] * (y_a @ w_branch_a) + g[..., 1, :] * (y_b @ w_branch_b)
    return mixed @ w_out

def route(xr, w_router, router_bias):
    f32 = jnp.float32
    scores = jax.nn.sigmoid(xr.astype(f32) @ w_router.astype(f32))
    sel = scores + router_bias.astype(f32)
    grp = sel.reshape(sel.shape[0], N_GROUPS, N_EXPERTS // N_GROUPS)
    grp_score = lax.top_k(grp, GROUP_SCORE_TOPK)[0].sum(-1)
    _, gidx = lax.top_k(grp_score, TOPK_GROUPS)
    gmask = jax.nn.one_hot(gidx, N_GROUPS, dtype=f32).sum(-2) > 0
    emask = jnp.repeat(gmask, N_EXPERTS // N_GROUPS, axis=-1)
    _, eidx = lax.top_k(jnp.where(emask, sel, -jnp.inf), TOP_K)
    w = jnp.take_along_axis(scores, eidx, axis=-1)
    w = w / w.sum(-1, keepdims=True) * ROUTED_SCALE
    return jnp.sum(jax.nn.one_hot(eidx, N_EXPERTS, dtype=f32) * w[..., None], axis=-2)

def moe_ffn(x, w_router, router_bias, w_eg, w_eu, w_ed, w_sg, w_su, w_sd):
    def per_row(xr):
        gate = route(xr, w_router, router_bias).astype(xr.dtype)
        hg = jnp.einsum('sd,edf->sef', xr, w_eg)
        hu = jnp.einsum('sd,edf->sef', xr, w_eu)
        h = jax.nn.silu(hg) * hu * gate[..., None]
        routed = jnp.einsum('sef,efd->sd', h, w_ed)
        shared = (jax.nn.silu(xr @ w_sg) * (xr @ w_su)) @ w_sd
        return routed + shared
    return lax.map(per_row, x)

def setup_inputs(seed: int = 0) -> dict:
    key = jax.random.key(seed)
    ks = jax.random.split(key, 32)

    def nrm(k, shape, scale):
        return jax.random.normal(k, shape, jnp.float32) * scale

    H = MLSTM_HEADS
    return {
        'x': nrm(ks[0], (BATCH, SEQ, D_MODEL), 1.0),
        'p': nrm(ks[1], (DEPTH, BATCH, SEQ, PLE_DIM), 1.0),
        'w_in': nrm(ks[2], (DEPTH, D_MODEL, IN_WIDTH), D_MODEL ** -0.5),
        'conv_w': nrm(ks[3], (DEPTH, CONV_K, CONV_WIDTH), CONV_K ** -0.5),
        'b_igate': nrm(ks[4], (DEPTH, H), 0.1),
        'b_fgate': jnp.linspace(3.0, 6.0, H, dtype=jnp.float32)[None, :] + nrm(ks[5], (DEPTH, H), 0.1),
        'mlstm_norm_g': 1.0 + nrm(ks[6], (DEPTH, MLSTM_V_W), 0.02),
        'w_branch_a': nrm(ks[7], (DEPTH, CONV_WIDTH, D_MODEL), BETA * CONV_WIDTH ** -0.5),
        'w_branch_b': nrm(ks[8], (DEPTH, MLSTM_V_W, D_MODEL), BETA * MLSTM_V_W ** -0.5),
        'w_out': nrm(ks[9], (DEPTH, D_MODEL, D_MODEL), BETA * D_MODEL ** -0.5),
        'ln1_g': 1.0 + nrm(ks[10], (DEPTH, D_MODEL), 0.02),
        'ln1_b': nrm(ks[11], (DEPTH, D_MODEL), 0.02),
        'w_router': nrm(ks[12], (DEPTH, D_MODEL, N_EXPERTS), D_MODEL ** -0.5),
        'router_bias': nrm(ks[13], (DEPTH, N_EXPERTS), 0.01),
        'w_exp_gate': nrm(ks[14], (DEPTH, N_EXPERTS, D_MODEL, D_EXPERT), D_MODEL ** -0.5),
        'w_exp_up': nrm(ks[15], (DEPTH, N_EXPERTS, D_MODEL, D_EXPERT), D_MODEL ** -0.5),
        'w_exp_down': nrm(ks[16], (DEPTH, N_EXPERTS, D_EXPERT, D_MODEL), BETA * D_EXPERT ** -0.5),
        'w_sh_gate': nrm(ks[17], (DEPTH, D_MODEL, D_SHARED), D_MODEL ** -0.5),
        'w_sh_up': nrm(ks[18], (DEPTH, D_MODEL, D_SHARED), D_MODEL ** -0.5),
        'w_sh_down': nrm(ks[19], (DEPTH, D_SHARED, D_MODEL), BETA * D_SHARED ** -0.5),
        'w_ple_gate': nrm(ks[20], (DEPTH, D_MODEL, D_MODEL), D_MODEL ** -0.5),
        'w_ple_proj': nrm(ks[21], (DEPTH, PLE_DIM, D_MODEL), BETA * PLE_DIM ** -0.5),
        'ln2_g': 1.0 + nrm(ks[22], (DEPTH, D_MODEL), 0.02),
        'ln2_b': nrm(ks[23], (DEPTH, D_MODEL), 0.02),
    }

def reference(x, p, w_in, conv_w, b_igate, b_fgate, mlstm_norm_g, w_branch_a, w_branch_b,
              w_out, ln1_g, ln1_b, w_router, router_bias, w_exp_gate, w_exp_up, w_exp_down,
              w_sh_gate, w_sh_up, w_sh_down, w_ple_gate, w_ple_proj, ln2_g, ln2_b):
    for i in range(DEPTH):
        h = hybrid_mixer(x, w_in[i], conv_w[i], b_igate[i], b_fgate[i], mlstm_norm_g[i],
                         w_branch_a[i], w_branch_b[i], w_out[i])
        x = layer_norm(ALPHA * x + h, ln1_g[i], ln1_b[i])
        y = moe_ffn(x, w_router[i], router_bias[i], w_exp_gate[i], w_exp_up[i], w_exp_down[i],
                    w_sh_gate[i], w_sh_up[i], w_sh_down[i])
        ple = jax.nn.sigmoid(x @ w_ple_gate[i]) * (p[i] @ w_ple_proj[i])
        x = layer_norm(ALPHA * x + y + ple, ln2_g[i], ln2_b[i])
    return x


_drawn_inputs = setup_inputs


def setup_inputs(seed=0):
    import zlib

    import numpy as np

    out = dict(_drawn_inputs(seed))
    spreads = {}
    factors = {'b_igate': 64.0, 'mlstm_norm_g': 4.488, 'ln2_g': 7.997, 'ln2_b': 8.225}
    for name, (base, spread) in spreads.items():
        noise = np.random.default_rng([zlib.crc32(name.encode()), seed]).standard_normal(out[name].shape)
        drawn = base * np.exp(spread * noise) if base else spread * noise
        out[name] = __import__('jax').numpy.asarray(drawn.astype(out[name].dtype))
    for name, factor in factors.items():
        out[name] = (out[name] * factor).astype(out[name].dtype)
    return out
```

```python
from contextlib import ExitStack

import concourse.bass as bass
from concourse import mybir

F32 = mybir.dt.float32
F32R = mybir.dt.float32r
I32 = mybir.dt.int32
BF16 = mybir.dt.bfloat16
ALU = mybir.AluOpType
ACT = mybir.ActivationFunctionType
AX_X = mybir.AxisListType.X

P = 128
KB = 1024


class Chain:

    def __init__(self, eng, sem):
        self.eng, self.sem, self.base, self.step = eng, sem, 0, 0

    def link(self, ins):
        ins.then_inc(self.sem, 1)
        self.step += 1
        self.eng.wait_ge(self.sem, self.base + self.step)

    def enter_loop(self, i, per_turn):
        self.start, self.per_turn = self.step, per_turn
        self.base = per_turn * i

    def leave_loop(self, turns):
        assert self.step - self.start == self.per_turn, (self.step - self.start, self.per_turn)
        self.base, self.step = 0, self.start + turns * self.per_turn


class Turn:

    def __init__(self, n0, k, i):
        assert n0 % 3 == 0 and k % 3 == 0
        self.n0, self.k, self.i = n0, k, i

    def piece(self, s):
        return self.n0 + self.k * self.i + s

    def third(self, s):
        return self.n0 // 3 + (self.k // 3) * self.i + s // 3

    def tile(self, t):
        return t % 3, 2 * self.n0 // 3 + (2 * self.k // 3) * self.i + t // 3


class Expert:

    def __init__(self, i, par):
        self.i, self.par = i, par
        self.e = 2 * i + par

    def next(self):
        return Expert(self.i + self.par, 1 - self.par)

    def last(self):
        return Expert(self.i - (1 - self.par), 1 - self.par)


def run_experts(eng, step, count):
    step(Expert(0, 0), False, True, True)
    step(Expert(0, 1), True, True, True)
    step(Expert(1, 0), True, True, True)
    with eng.Fori(1, count // 2 - 2) as i:
        step(Expert(i, 1), True, True, True)
        step(Expert(i + 1, 0), True, True, True)
    step(Expert(count // 2 - 2, 1), True, True, True)
    step(Expert(count // 2 - 1, 0), True, True, False)
    step(Expert(count // 2 - 1, 1), True, False, False)
    step(Expert(count // 2, 0), True, False, False)


def hybrid_layer(nc, x, p, w_in, conv_w, b_igate, b_fgate, norm_g, w_a, w_b, w_out, ln1_g, ln1_b,
                 w_router, router_bias, w_eg, w_eu, w_ed, w_sg, w_su, w_sd, w_pg, w_pp, ln2_g, ln2_b, out):
    _, SEQ, D = x.shape
    HEADS = b_igate.shape[1]
    DH = norm_g.shape[1] // HEADS
    PLE = p.shape[3]
    E = w_eg.shape[1]
    F = w_eg.shape[3]
    NT = SEQ // P
    KD = D // P
    KF = F // P
    ALPHA = 2.0 ** 0.25
    TOP_K, TOP_GROUPS, ROUTED_SCALE = 8, 4, 2.5
    OOB = 4096
    LOW = 1e30
    QK_SCALE = float(DH) ** -0.5
    RMS_EPS, LN_EPS = 1e-6, 1e-5
    assert SEQ == 512 and D == 1024 and DH == P and HEADS == KD and PLE == F == 256 and NT == 4

    COLS = 256
    COL = {n: j * 1024 for j, n in enumerate(["c_in", "c_out", "c_val", "q", "k", "v", "o"])}
    GATES = 7 * 1024
    MERGE = GATES + 2 * HEADS
    SEG = [0, 512, 896, 1152]
    SEGW = 1280

    x_tok = x[0].rearrange("(t p) d -> p t d", p=P)
    p_tok = p[0, 0].rearrange("(t p) d -> p t d", p=P)

    def by_row(w):
        return w.rearrange("(p k) n -> p k n", p=P)

    def by_tile(w):
        return w.rearrange("(k p) n -> p k n", p=P)

    win_r = by_row(w_in[0])
    wa_t, wb_t, wo_t = by_tile(w_a[0]), by_tile(w_b[0]), by_tile(w_out[0])
    wpp_r = by_row(w_pp[0])

    with ExitStack() as ctx:
        def sem(name):
            return ctx.enter_context(nc.semaphore(name))

        base = (nc.sbuf_base + 63) // 64 * 64

        def at(name, kb, shape, dt=F32):
            return nc.alloc_sbuf_tensor_at(name, shape, dt, offset=base + int(kb * KB))

        split_hi = at("split_hi", 0, [P, 3, 2048], F32R)
        split_lo = at("split_lo", 24, [P, 3, 2048], F32R)
        raw = at("raw", 48, [P, 6, 2048])
        decay = at("decay", 72, [P, 2, SEGW])
        head_out = at("head_out", 82, [P, NT, DH])
        conv_u = at("conv_u", 84, [P, 2, SEQ + 2])
        conv_c = at("conv_c", 88.5, [P, 2, SEQ])
        mixed_a = at("mixed_a", 72, [P, KD, SEQ])
        branch = at("branch", 88, [P, 2, SEQ])
        merge_g = at("merge_g", 92, [P, 2, SEQ])
        R = 96
        xT_hi = at("xT_hi", R, [P, KD, SEQ], F32R)
        xT_lo = at("xT_lo", R + 16, [P, KD, SEQ], F32R)
        yaT_hi = at("yaT_hi", R + 32, [P, KD, SEQ], F32R)
        yaT_lo = at("yaT_lo", R + 48, [P, KD, SEQ], F32R)
        hT = at("hT", R + 64, [P, HEADS, SEQ])
        ybT_hi = at("ybT_hi", R + 64, [P, KD, SEQ], F32R)
        ybT_lo = at("ybT_lo", R + 80, [P, KD, SEQ], F32R)
        qT = at("qT", R + 80, [P, 2, SEQ])
        kT = at("kT", R + 84, [P, 2, SEQ])
        v_ext = at("v_ext", R + 88, [P, NT, 2, DH + 2])
        run_max = at("run_max", R + 93, [HEADS, SEQ])
        pT_hi = at("pT_hi", R + 96, [P, KF, SEQ], F32R)
        pT_lo = at("pT_lo", R + 100, [P, KF, SEQ], F32R)
        max_sel = at("max_sel", R + 104, [HEADS, 2, SEQ])
        yb_tmp = at("yb_tmp", R + 104, [P, 2, SEQ])
        C = R + 108
        ident = at("ident", C, [P, P])
        causal = at("causal", C + 0.5, [P, P])
        ones_f = at("ones_f", C + 1, [P, P])
        params = at("params", C + 1.5, [P, 32])
        g_tok = at("g_tok", C + 1.625, [P, NT, HEADS])
        guard = at("guard", C + 1.75, [P, NT, HEADS])
        hs = at("hs", C + 1.875, [P, 10, NT])
        bias_if = at("bias_if", C + 2.125, [HEADS, 2])
        one_col = at("one_col", C + 2.1875, [P, 1])
        x_in = at("x_in", R + 32, [P, NT, D])
        p_in = at("p_in", R + 48, [P, NT, PLE])
        gt = [at(f"gate_tmp{j}", R + 52 + 2 * j, [HEADS, SEQ]) for j in range(6)]
        wg_raw = at("wg_raw", R + 64, [P, KD, 2 * HEADS])
        wg_hi = at("wg_hi", R + 65, [P, KD, 2 * HEADS], F32R)
        wg_lo = at("wg_lo", R + 66, [P, KD, 2 * HEADS], F32R)
        gate_tok = at("gate_tok", R + 67, [P, NT, 2 * HEADS])
        param_rows = at("param_rows", R + 68, [32, P])
        ple_proj = at("ple_proj", R + 32, [P, NT, D])
        mix_hi = at("mix_hi", R + 48, [P, KD, SEQ], F32R)
        mix_lo = at("mix_lo", 72, [P, KD, SEQ], F32R)

        x1 = at("x1", R, [P, NT, D])
        y_acc = at("y_acc", R + 16, [P, NT, D])
        ln_g = at("ln_g", 88, [P, D])
        ln_b = at("ln_b", 92, [P, D])
        x1T_hi = at("x1T_hi", R + 64, [P, KD, SEQ], F32R)
        x1T_lo = at("x1T_lo", R + 80, [P, KD, SEQ], F32R)
        T = R + 48
        scores_s = at("scores_s", T, [P, NT, E])
        sel = at("sel", T + 1, [P, NT, E])
        top_g = at("top_g", T + 2, [P, NT * 8, 8])
        cmp_gt = at("cmp_gt", T + 3, [P, NT, 8, 8])
        cmp_eq = at("cmp_eq", T + 4, [P, NT, 8, 8])
        before = at("before", T + 5, [P, 8, 8])
        r_bias = at("r_bias", R + 104, [P, E])
        gsc = at("gsc", T + 5.5, [P, NT, 8])
        gcnt = at("gcnt", T + 5.625, [P, NT, 8])
        gmask = at("gmask", T + 5.75, [P, NT, 8])
        top8 = at("top8", T + 5.875, [P, NT, 8])
        cand = at("cand", T + 6, [P, NT, E])
        rest = at("rest", T + 7, [P, NT, E])
        chosen = at("chosen", T + 8, [P, NT, E])
        chosen_b = at("chosen_b", T + 9, [P, NT, E], BF16)
        wsel = at("wsel", T + 10, [P, NT, E])
        rank = at("rank", T + 11, [P, NT, E])
        wsum = at("wsum", T + 12, [P, 2, NT])
        sh_s = at("sh_s", T + 12.25, [P, F])
        sh_h = [at(f"sh_h{j}", 76 + j, [P, F]) for j in range(4)]
        shT_hi = at("shT_hi", 84, [P, KF, SEQ], F32R)
        shT_lo = at("shT_lo", 80, [P, KF, SEQ], F32R)
        ple_s = at("ple_s", R + 104, [P, 2, 512])
        route_cols = at("route_cols", R + 96, [P, NT, E + 2, 4], F32R)
        slot_of = at("slot_of", R + 100.25, [P, NT, E + 2])
        one_hot = at("one_hot", R + 101.3125, [P, NT, P], F32R)
        ex_h = at("ex_h", R + 104, [P, F])
        exT_hi = at("exT_hi", R + 105, [P, KF, P], F32R)
        exT_lo = at("exT_lo", R + 106, [P, KF, P], F32R)
        split_hi_b = at("split_hi_b", R + 32, [P, 3, 2048], F32R)
        split_lo_b = at("split_lo_b", R + 56, [P, 3, 2048], F32R)
        xg = [at(f"xg{b}", R + 4 * b, [P, D]) for b in range(2)]
        xgT_hi = [at(f"xgT_hi{b}", R + 8 + 80 * b, [P, KD, P], F32R) for b in range(2)]
        xgT_lo = [at(f"xgT_lo{b}", R + 12 + 80 * b, [P, KD, P], F32R) for b in range(2)]
        y_out = [at(f"y_out{b}", R + 80 + 4 * b, [P, D]) for b in range(2)]
        iota_row = at("iota_row", C + 2.25, [P, P])
        lower_b = at("lower_b", C + 2.75, [P, P], BF16)
        ones_b = at("ones_b", C + 3, [P, P], BF16)
        o = C + 3.25
        tok_id = at("tok_id", o, [P, 2, NT])
        tok_idx = [at(f"tok_idx{b}", o + 0.0625 * (1 + b), [P, 1], I32) for b in range(2)]
        dst_idx = [at(f"dst_idx{b}", o + 0.0625 * (3 + b), [P, 1], I32) for b in range(2)]
        ln_s = at("ln_s", C + 3.5625, [P, 8, NT])
        counts = at("counts", C + 3.6875, [P, 2])
        counts_i = at("counts_i", C + 3.71875, [P, 1], I32)
        bn = at("bn", C + 3.75, [P, 2, 6])
        bn_mv = at("bn_mv", C + 3.8125, [P, NT, 2])
        dst_all = at("dst_all", R + 103.3125, [P, E + 2])
        gate_all = at("gate_all", R + 103.59375, [P, E + 2])
        iota_i = at("iota_i", R + 80, [P, P], I32)
        iota_s = at("iota_s", R + 81, [P, 8, 8], I32)
        iota_t = at("iota_t", R + 82, [P, 2, NT], I32)
        parts = [at(f"parts{j}", 32 * j, [P, 8, D]) for j in range(3)]
        tail_s = [at(f"tail_s{j}", R + 32 + 4 * j, [P, D]) for j in range(4)]
        x1_dram = nc.dram_tensor("x1_rows", (SEQ, D), F32, kind="Internal").ap()
        y_dram = nc.dram_tensor("expert_rows", (TOP_K * SEQ, D), F32, kind="Internal").ap()

        bank = [ctx.enter_context(nc.psum_tensor(f"bank{i}", [P, 512], F32)) for i in range(8)]
        MB, S0, S13, S2, NUM = bank[6], bank[3], bank[4], bank[5], bank[7]
        S_PLACE = [(S0, 0), (S13, 0), (S2, 0), (S13, 384)]
        NUM_PLACE = [(NUM, 0), (NUM, 130), (NUM, 260), (S2, 256)]

        consts_made = sem("consts_made")
        x_loaded = sem("x_loaded")
        p_loaded = sem("p_loaded")
        small_loaded = sem("small_loaded")
        raw_full = [sem(f"raw_full{j}") for j in range(6)]
        hi_done = sem("hi_done")
        lo_done = sem("lo_done")
        acc_full = [sem(f"acc_full{j}") for j in range(3)]
        acc_free = [sem(f"acc_free{j}") for j in range(3)]
        xT_ready = sem("xT_ready")
        xT_hi_done = sem("xT_hi_done")
        xT_lo_done = sem("xT_lo_done")
        wg_split = sem("wg_split")
        gates_ready = sem("gates_ready")
        gates_used = sem("gates_used")
        gate_fn = sem("gate_fn")
        gate_step = sem("gate_step")
        dve_chain = sem("dve_chain")
        pool_chain = sem("pool_chain")
        sel_done = sem("sel_done")
        mb_ready = sem("mb_ready")
        arg_done = sem("arg_done")
        exp_done = sem("exp_done")
        mask_done = sem("mask_done")
        s_ready = sem("s_ready")
        pt_done = sem("pt_done")
        num_ready = sem("num_ready")
        sq_done = sem("sq_done")
        ln_in = sem("ln_in")
        ln_out = sem("ln_out")
        head_done = sem("head_done")
        tr_ready = sem("tr_ready")
        tr_done = sem("tr_done")
        ya_hi_done = sem("ya_hi_done")
        ya_lo_done = sem("ya_lo_done")
        mixa_done = sem("mixa_done")
        yb_done = sem("yb_done")
        ybh_done = sem("ybh_done")
        ybl_done = sem("ybl_done")
        mix_done = sem("mix_done")
        mixh_done = sem("mixh_done")
        mixl_done = sem("mixl_done")
        loads_issued = sem("loads_issued")
        rounds_over = sem("rounds_over")
        over_done = sem("over_done")
        over_loaded = sem("over_loaded")
        over_hi = sem("over_hi")
        over_lo = sem("over_lo")
        over_hot = sem("over_hot")
        over_lists_ready = sem("over_lists_ready")
        over_lists = sem("over_lists")
        over_shifted = sem("over_shifted")
        over_gathered = sem("over_gathered")
        over_turned = sem("over_turned")
        over_xh = sem("over_xh")
        over_xl = sem("over_xl")
        over_gu = sem("over_gu")
        over_silu = sem("over_silu")
        over_h = sem("over_h")
        over_exT = sem("over_exT")
        over_exh = sem("over_exh")
        over_exl = sem("over_exl")
        over_y = sem("over_y")
        over_copied = sem("over_copied")
        over_scattered = sem("over_scattered")
        ple_ready = [sem(f"ple_ready{j}") for j in range(3)]
        part_loaded = [sem(f"part_loaded{j}") for j in range(4)]
        y_free = sem("y_free")
        lists_written = sem("lists_written")
        ln_loaded = sem("ln_loaded")
        x1_loaded = sem("x1_loaded")
        rb_loaded = sem("rb_loaded")
        ln2_loaded = sem("ln2_loaded")
        x1_stored = sem("x1_stored")
        out_stored = sem("out_stored")
        seed_in = sem("seed_in")
        seed_out = sem("seed_out")
        x1_norm = sem("x1_norm")
        x1_done = sem("x1_done")
        x1T_ready = sem("x1T_ready")
        x1T_hi_done = sem("x1T_hi_done")
        x1T_lo_done = sem("x1T_lo_done")
        y_init = sem("y_init")
        router_ready = sem("router_ready")
        scores_done = sem("scores_done")
        chosen_done = sem("chosen_done")
        pos_ready = sem("pos_ready")
        sh_ready = sem("sh_ready")
        sh_silu = sem("sh_silu")
        sh_done = sem("sh_done")
        shT_ready = sem("shT_ready")
        shT_hi_done = sem("shT_hi_done")
        shT_lo_done = sem("shT_lo_done")
        shd_ready = sem("shd_ready")
        shd_done = sem("shd_done")
        ple_sig = sem("ple_sig")
        ple_done = sem("ple_done")
        tables_done = sem("tables_done")
        hot_done = sem("hot_done")
        idx_ready = sem("idx_ready")
        idx_done = sem("idx_done")
        dst_done = sem("dst_done")
        gathered0 = sem("gathered0")
        gathered1 = sem("gathered1")
        scattered0 = sem("scattered0")
        scattered1 = sem("scattered1")
        xgT_ready = sem("xgT_ready")
        xgTh_done = sem("xgTh_done")
        xgTl_done = sem("xgTl_done")
        gu_ready = sem("gu_ready")
        silu_done = sem("silu_done")
        h_done = sem("h_done")
        exT_ready = sem("exT_ready")
        exTh_done = sem("exTh_done")
        exTl_done = sem("exTl_done")
        y_ready = sem("y_ready")
        y_done = sem("y_done")
        pool_tick = sem("pool_tick")
        iota_done = sem("iota_done")
        xg_clear = sem("xg_clear")
        part_done = sem("part_done")
        out_done = sem("out_done")

        def further_rounds(eng, block_of, before=None):
            eng.wait_ge(tables_done, 1)
            load_max = eng.value_load(counts_i[0:1, 0:1], min_val=0, max_val=SEQ)
            for r in range(1, NT):
                with eng.If(load_max > P * r):
                    if before:
                        before(r)
                    with eng.Fori(0, E) as e:
                        block_of(e, r, e + (E * (r - 1) + 1))

        block = ctx.enter_context(nc.Block())

        @block.sync
        def _(sp):
            sp.dma_start(x_in[:], x_tok).then_inc(x_loaded, 16)
            sp.dma_start(wg_raw[:], win_r[:, :, GATES:GATES + 2 * HEADS]).then_inc(small_loaded, 16)
            sp.dma_start(param_rows[0:24, :], conv_w[0].rearrange("j (m c) -> (j m) c", c=P)).then_inc(small_loaded, 16)
            sp.dma_start(param_rows[24:32, :], norm_g[0].rearrange("(m c) -> m c", c=P)).then_inc(small_loaded, 16)
            sp.dma_start(bias_if[:, 0:1], b_igate[0].rearrange("(h a) -> h a", a=1)).then_inc(small_loaded, 16)
            sp.dma_start(bias_if[:, 1:2], b_fgate[0].rearrange("(h a) -> h a", a=1)).then_inc(small_loaded, 16)

            def load(turn, s, src, cols=None, slots=3):
                n = turn.piece(s)
                slot = s % 3
                if not isinstance(n, int):
                    sp.wait_ge(lo_done, n - 2)
                    sp.sem_inc(loads_issued, 1)
                elif n >= 3:
                    sp.wait_ge(lo_done, n - 2)
                dst = raw[:, slot, 0:src.shape[1] * src.shape[2]].rearrange("p (k n) -> p k n", k=src.shape[1])
                sp.dma_start(dst, src).then_inc(raw_full[slot], 16)

            def cols_of(w, first, i):
                return w[:, :, bass.ds(first + COLS * i, COLS)]

            def load_a(i):
                t = Turn(0, 6, i)
                for s, name in enumerate(["q", "k", "v", "c_in", "c_val", "c_out"]):
                    load(t, s, cols_of(win_r, COL[name], i))

            load_a(0)
            sp.dma_start(p_in[:], p_tok).then_inc(p_loaded, 16)
            with sp.Fori(1, 4) as i:
                load_a(i)
            with sp.Fori(0, 4) as i:
                t = Turn(24, 3, i)
                load(t, 0, cols_of(wa_t, 0, i))
                load(t, 1, cols_of(win_r, MERGE, i))
                load(t, 2, cols_of(win_r, COL["o"], i))
            with sp.Fori(0, 4) as i:
                t = Turn(36, 3, i)
                load(t, 0, cols_of(wpp_r, 0, i))
                load(t, 1, cols_of(win_r, MERGE + D, i))
                load(t, 2, cols_of(wb_t, 0, i))
            b, use = Turn(45, 3, 0).tile(3)
            sp.wait_ge(acc_full[b], use + 1)
            sp.dma_start(x1[:], x_tok).then_inc(x1_loaded, 16)
            sp.dma_start(r_bias[:], router_bias[0:1, :].broadcast_to([P, E])).then_inc(rb_loaded, 16)

            def load_at(n, src, slot):
                if n >= 3:
                    sp.wait_ge(lo_done, n - 2)
                dst = raw[:, slot, 0:src.shape[1] * src.shape[2]].rearrange("p (k n) -> p k n", k=src.shape[1])
                sp.dma_start(dst, src).then_inc(raw_full[slot], 16)

            for n in range(4):
                load_at(48 + n, wo_t[:, :, COLS * n:COLS * (n + 1)], n % 3)
                if n == 2:
                    sp.wait_ge(mixl_done, KD)
                    sp.dma_start(ln_g[:], ln1_g[0:1, :].broadcast_to([P, D])).then_inc(ln_loaded, 16)
                    sp.dma_start(ln_b[:], ln1_b[0:1, :].broadcast_to([P, D])).then_inc(ln_loaded, 16)
            load_at(52, by_row(w_router[0]), 1)
            load_at(53, by_row(w_sd[0]), 2)
            load_at(54, by_row(w_sg[0]), 0)
            for tt in range(NT):
                sp.wait_ge(x1_done, tt + 1)
                sp.dma_start(x1_dram[P * tt:P * (tt + 1), :], x1[:, tt, :]).then_inc(x1_stored, 16)
            load_at(55, by_row(w_su[0]), 1)
            for n in range(4):
                load_at(56 + n, by_row(w_pg[0])[:, :, COLS * n:COLS * (n + 1)], (56 + n) % 3)

            def load_expert(i, b, first=False):
                e = 2 * i + b
                for s, w in enumerate((w_eg, w_eu, w_ed)):
                    n = 60 + 3 * e + s
                    back = 2 if first and b == 0 else 5
                    sp.wait_ge(lo_done, n - back)
                    if not isinstance(i, int):
                        sp.sem_inc(loads_issued, 1)
                    src = w[0].rearrange("e (p k) n -> p e (k n)", p=P)[:, bass.ds(e, 1), :]
                    sp.dma_start(raw[:, 3 * b + s:3 * b + s + 1, :], src).then_inc(raw_full[3 * b + s], 16)

            for b in range(2):
                load_expert(0, b, first=True)
            with sp.Fori(1, E // 2) as i:
                for b in range(2):
                    load_expert(i, b)

            sp.wait_ge(y_ready, E)
            sp.dma_start(tail_s[0][:], ln2_g[0:1, :].broadcast_to([P, D])).then_inc(ln2_loaded, 16)
            sp.dma_start(tail_s[1][:], ln2_b[0:1, :].broadcast_to([P, D])).then_inc(ln2_loaded, 16)
            sp.wait_ge(y_free, 2 + E)
            def over_sp(e, r, n):
                for s, w in enumerate((w_eg, w_eu, w_ed)):
                    sp.wait_ge(over_done, n)
                    sp.sem_inc(loads_issued, 1)
                    src = w[0].rearrange("e (p k) n -> p e (k n)", p=P)[:, bass.ds(e, 1), :]
                    sp.dma_start(raw[:, s:s + 1, :], src).then_inc(over_loaded, 16)

            further_rounds(sp, over_sp)
            sp.wait_ge(rounds_over, 1)
            rows = y_dram.rearrange("(t p k) d -> t p k d", t=NT, p=P)
            for tt in range(NT):
                if tt == 3:
                    sp.wait_ge(part_done, 1)
                sp.dma_start(parts[tt % 3][:], rows[tt]).then_inc(part_loaded[tt], 16)
            out_tok = out[0].rearrange("(t p) d -> p t d", p=P)
            for tt in range(NT):
                sp.wait_ge(out_done, tt + 1)
                sp.dma_start(out_tok[:, tt, :], y_acc[:, tt, :]).then_inc(out_stored, 16)
            sp.wait_ge(out_stored, 16 * NT)

        @block.gpsimd
        def _(pool):
            ch = Chain(pool, pool_chain)
            nc.gpsimd.memset(one_col[:], 1.0).then_inc(consts_made, 1)
            ch.link(nc.gpsimd.memset(ones_f[:], 1.0))
            ch.link(nc.gpsimd.memset(ident[:], 0.0))
            nc.gpsimd.affine_select(out=ident[:], in_=ident[:], compare_op=ALU.not_equal, fill=1.0, base=0,
                                    pattern=[[-1, P]], channel_multiplier=1).then_inc(consts_made, 1)
            nc.gpsimd.affine_select(out=causal[:], in_=ones_f[:], compare_op=ALU.is_ge, fill=0.0, base=0,
                                    pattern=[[1, P]], channel_multiplier=-1).then_inc(consts_made, 1)
            pool.wait_ge(consts_made, 5)
            with pool.Fori(0, 4) as i:
                for hl in range(2):
                    for a in range(NT):
                        if a == 0:
                            pool.wait_ge(exp_done, 2 * i + hl + 1)
                        blk = decay[:, hl, SEG[a]:SEG[a] + P]
                        nc.gpsimd.tensor_tensor(blk, blk, causal[:], ALU.mult).then_inc(mask_done, 1)
            pool.wait_ge(mixl_done, KD)
            nc.gpsimd.iota(iota_i[:], pattern=[[1, P]], base=0, channel_multiplier=0).then_inc(iota_done, 1)
            nc.gpsimd.iota(iota_s[:], pattern=[[1, 8], [-1, 8]], base=0, channel_multiplier=0).then_inc(iota_done, 1)
            nc.gpsimd.iota(iota_t[:, 0, :], pattern=[[P, NT]], base=-OOB, channel_multiplier=1).then_inc(iota_done, 1)
            nc.gpsimd.iota(iota_t[:, 1, :], pattern=[[TOP_K * P, NT]], base=-OOB, channel_multiplier=TOP_K).then_inc(iota_done, 1)
            for tt in range(NT):
                pool.wait_ge(x1_norm, tt + 1)
                nc.gpsimd.tensor_tensor(x1[:, tt, :], x1[:, tt, :], ln_b[:], ALU.add).then_inc(x1_done, 1)
            pool.wait_ge(x1_stored, 16 * NT)
            pool.wait_ge(x1T_ready, KD)
            pool.wait_ge(y_init, NT)
            for b in range(2):
                nc.gpsimd.memset(xg[b][:], 0.0).then_inc(xg_clear, 1)
            gathered, scattered = (gathered0, gathered1), (scattered0, scattered1)

            def gather(b):
                nc.gpsimd.indirect_dma_start(out=xg[b][:], out_offset=None, in_=x1_dram,
                                             in_offset=bass.IndirectOffsetOnAxis(ap=tok_idx[b][:, 0:1], axis=0),
                                             bounds_check=SEQ - 1, oob_is_err=False).then_inc(gathered[b], 16)

            def scatter(b):
                nc.gpsimd.indirect_dma_start(out=y_dram, in_=y_out[b][:], in_offset=None,
                                             out_offset=bass.IndirectOffsetOnAxis(ap=dst_idx[b][:, 0:1], axis=0),
                                             bounds_check=TOP_K * SEQ - 1, oob_is_err=False).then_inc(scattered[b], 16)

            pool.wait_ge(xg_clear, 2)
            pool.sem_inc(y_free, 1)
            for b in range(2):
                pool.wait_ge(idx_done, b + 1)
                gather(b)

            def expert_pool(x, back, ahead, tables):
                if tables:
                    pool.wait_ge(idx_done, x.e + 3)
                    pool.wait_ge(xgT_ready, x.e + 1)
                    pool.sem_inc(pool_tick, 1)
                    gather(x.par)
                if back:
                    if not (isinstance(x.i, int) and x.i == 0):
                        pool.wait_ge(scattered[x.par], 16 * x.i)
                    pool.sem_inc(y_free, 1)
                    pool.wait_ge(dst_done, x.e)
                    pool.wait_ge(y_done, 2 * x.e + 1)
                    pool.sem_inc(pool_tick, 1)
                    scatter(1 - x.par)

            run_experts(pool, expert_pool, E)
            pool.wait_ge(scattered1, 16 * (E // 2))
            pool.sem_inc(y_free, 1)

            def over_pool(e, r, n):
                pool.wait_ge(over_lists, n)
                pool.wait_ge(over_done, n)
                pool.sem_inc(pool_tick, 1)
                nc.gpsimd.indirect_dma_start(out=xg[0][:], out_offset=None, in_=x1_dram,
                                             in_offset=bass.IndirectOffsetOnAxis(ap=tok_idx[0][:, 0:1], axis=0),
                                             bounds_check=SEQ - 1, oob_is_err=False).then_inc(over_gathered, 16)
                pool.wait_ge(over_copied, 2 * n)
                pool.sem_inc(pool_tick, 1)
                nc.gpsimd.indirect_dma_start(out=y_dram, in_=y_out[0][:], in_offset=None,
                                             out_offset=bass.IndirectOffsetOnAxis(ap=dst_idx[0][:, 0:1], axis=0),
                                             bounds_check=TOP_K * SEQ - 1, oob_is_err=False).then_inc(over_scattered, 16)
                pool.wait_ge(over_scattered, 16 * n)
                pool.sem_inc(over_done, 1)

            pool.sem_inc(over_done, 1)
            further_rounds(pool, over_pool)
            pool.sem_inc(rounds_over, 1)

        @block.scalar
        def _(act):
            def hi(turn, s):
                slot = s % 3
                n = turn.piece(s)
                act.wait_ge(raw_full[slot], 16 * (turn.third(s) + 1))
                if not (isinstance(n, int) and n < 3):
                    b, use = turn.tile(2 * (s - 3) + 1)
                    act.wait_ge(acc_full[b], use + 1)
                nc.scalar.activation(split_hi[:, slot, :], raw[:, slot, :], ACT.Copy).then_inc(hi_done, 1)

            act.sem_inc(tr_done, 1)
            act.sem_inc(y_done, 1)
            for kk in range(KD):
                act.wait_ge(xT_ready, kk + 1)
                nc.scalar.activation(xT_hi[:, kk, :], bank[kk][:], ACT.Copy).then_inc(xT_hi_done, 1)
                if kk == 0:
                    act.wait_ge(small_loaded, 16 * 5)
                    nc.scalar.activation(wg_hi[:], wg_raw[:], ACT.Copy).then_inc(wg_split, 1)
            for s in range(3):
                hi(Turn(0, 3, 0), s)
            for kk in range(KF):
                act.wait_ge(xT_ready, KD + kk + 1)
                nc.scalar.activation(pT_hi[:, kk, :], bank[kk][:], ACT.Copy).then_inc(xT_hi_done, 1)
            act.wait_ge(gate_step, 1)
            nc.scalar.activation(gt[2][:], gt[2][:], ACT.Exp, scale=-1.0).then_inc(gate_fn, 1)
            act.wait_ge(gate_fn, 1)
            act.wait_ge(consts_made, 1)
            nc.scalar.activation(gt[2][:], gt[2][:], ACT.Ln, bias=one_col[0:HEADS, :]).then_inc(gate_fn, 1)
            act.wait_ge(gate_step, 2)
            nc.scalar.activation(gt[4][:], gt[4][:], ACT.Exp, scale=-1.0).then_inc(gate_fn, 1)

            with act.Fori(0, 4) as i:
                t = Turn(0, 6, i)

                def evac(tile, out_, free=True, **kw):
                    b, use = t.tile(tile)
                    act.wait_ge(acc_full[b], use + 1)
                    return nc.scalar.activation(out_, bank[b][:], ACT.Copy, **kw)

                for m in range(2):
                    evac(m, qT[:, m, :], scale=QK_SCALE).then_inc(acc_free[m % 3], 1)
                hi(t, 3)
                for m in range(2):
                    evac(2 + m, kT[:, m, :]).then_inc(acc_free[(2 + m) % 3], 1)
                hi(t, 4)
                hi(t, 5)

                def squares(hl):
                    act.wait_ge(num_ready, 2 * i + hl + 1)
                    for j in range(NT):
                        b, c0 = NUM_PLACE[j]
                        nc.scalar.activation(head_out[:, j, :], b[:, c0:c0 + DH], ACT.Square,
                                             accum_out=hs[:, 0, j:j + 1]).then_inc(sq_done, 1)

                def weights(hl):
                    act.wait_ge(arg_done, 8 * i + 4 * hl + 4)
                    nc.scalar.activation(decay[:, hl, :], decay[:, hl, :], ACT.Exp, scale=-1.0).then_inc(exp_done, 1)

                def rsqrt_seed(hl):
                    act.wait_ge(ln_in, 2 * i + hl + 1)
                    nc.scalar.activation(hs[:, 5, :], hs[:, 4, :], ACT.Ln).then_inc(ln_out, 1)
                    act.wait_ge(ln_out, 4 * i + 2 * hl + 1)
                    nc.scalar.activation(hs[:, 6, :], hs[:, 5, :], ACT.Exp, scale=-0.5).then_inc(ln_out, 1)

                def head_back(hl):
                    act.wait_ge(tr_ready, 2 * i + hl + 1)
                    nc.scalar.activation(hT[:, bass.ds(2 * i + hl, 1), :],
                                         MB[:].rearrange("p (a n) -> p a n", a=1), ACT.Copy).then_inc(tr_done, 1)

                def conv_gated(m):
                    b, use = t.tile(10 + m)
                    act.wait_ge(acc_free[b], use + 2)

                act.wait_ge(ya_lo_done, 2 * i + 1)
                evac(6, conv_c[:, 0, :]).then_inc(acc_free[0], 1)
                weights(0)
                evac(7, conv_c[:, 1, :]).then_inc(acc_free[1], 1)
                hi(t, 6)
                squares(0)
                rsqrt_seed(0)
                weights(1)
                hi(t, 7)
                head_back(0)
                conv_gated(0)
                nc.scalar.activation(yaT_hi[:, bass.ds(2 * i, 1), :], conv_c[:, 0:1, :], ACT.Copy).then_inc(ya_hi_done, 1)
                squares(1)
                rsqrt_seed(1)
                conv_gated(1)
                nc.scalar.activation(yaT_hi[:, bass.ds(2 * i + 1, 1), :], conv_c[:, 1:2, :], ACT.Copy).then_inc(ya_hi_done, 1)
                head_back(1)
                hi(t, 8)

            with act.Fori(0, 4) as i:
                t = Turn(24, 3, i)
                for m in range(2):
                    b, use = t.tile(m)
                    act.wait_ge(acc_full[b], use + 1)
                    act.wait_ge(mixa_done, 2 * i + m + 1)
                    nc.scalar.activation(branch[:, m, :], bank[b][:], ACT.Copy).then_inc(acc_free[b], 1)
                hi(t, 3)
                for m in range(2):
                    b, use = t.tile(2 + m)
                    act.wait_ge(acc_full[b], use + 1)
                    nc.scalar.activation(merge_g[:, m, :], bank[b][:], ACT.Sigmoid).then_inc(acc_free[b], 1)
                hi(t, 4)
                for m in range(2):
                    b, use = t.tile(4 + m)
                    act.wait_ge(acc_full[b], use + 1)
                    act.wait_ge(ybl_done, 2 * i + m + 1)
                    nc.scalar.activation(yb_tmp[:, m, :], bank[b][:], ACT.Sigmoid).then_inc(acc_free[b], 1)
                hi(t, 5)
                for m in range(2):
                    act.wait_ge(yb_done, 2 * i + m + 1)
                    nc.scalar.activation(ybT_hi[:, bass.ds(2 * i + m, 1), :], yb_tmp[:, m:m + 1, :], ACT.Copy).then_inc(ybh_done, 1)

            act.wait_ge(mixa_done, 2 + KD)
            with act.Fori(0, 4) as i:
                t = Turn(36, 3, i)
                for m in range(2):
                    b, use = t.tile(m)
                    act.wait_ge(acc_full[b], use + 1)
                    nc.scalar.activation(ple_proj[:, 2 * m:2 * m + 2, bass.ds(COLS * i, COLS)],
                                         bank[b][:].rearrange("p (t n) -> p t n", t=2), ACT.Copy).then_inc(acc_free[b], 1)
                hi(t, 3)
                for m in range(2):
                    b, use = t.tile(2 + m)
                    act.wait_ge(acc_full[b], use + 1)
                    nc.scalar.activation(merge_g[:, m, :], bank[b][:], ACT.Sigmoid).then_inc(acc_free[b], 1)
                hi(t, 4)
                for m in range(2):
                    act.wait_ge(mix_done, 2 * i + m + 1)
                    nc.scalar.activation(mix_hi[:, bass.ds(2 * i + m, 1), :], branch[:, m:m + 1, :], ACT.Copy).then_inc(mixh_done, 1)
                hi(t, 5)

            def hi_at(n, free=None, width=2048):
                act.wait_ge(raw_full[n % 3], 16 * (n // 3 + 1))
                if free:
                    act.wait_ge(*free)
                nc.scalar.activation(split_hi[:, n % 3, 0:width], raw[:, n % 3, 0:width], ACT.Copy).then_inc(hi_done, 1)

            def rsqrt_act(k):
                act.wait_ge(seed_in, k)
                nc.scalar.activation(ln_s[:, 1, :], ln_s[:, 0, :], ACT.Ln).then_inc(seed_out, 1)
                act.wait_ge(seed_out, 2 * k - 1)
                nc.scalar.activation(ln_s[:, 2, :], ln_s[:, 1, :], ACT.Exp, scale=-0.5).then_inc(seed_out, 1)

            out_turn = Turn(48, 12, 0)
            for s in range(4):
                b, use = out_turn.tile(2 * s + 1)
                hi_at(51 + s, (acc_full[b], use + 1), width=KD * E if s == 1 else 2048)
            rsqrt_act(1)
            for tt in range(NT):
                act.wait_ge(x1_done, tt + 1)
                nc.scalar.activation(y_acc[:, tt, :], x1[:, tt, :], ACT.Copy, scale=ALPHA).then_inc(y_init, 1)
            for kk in range(KD):
                act.wait_ge(x1T_ready, kk + 1)
                nc.scalar.activation(x1T_hi[:, kk, :], bank[3 + kk % 5][:], ACT.Copy).then_inc(x1T_hi_done, 1)
            hi_at(55, (router_ready, 1))
            nc.scalar.activation(scores_s[:].rearrange("p t e -> p (t e)"), bank[0][:, 0:NT * E], ACT.Sigmoid).then_inc(scores_done, 1)
            for tt in range(NT):
                act.wait_ge(sh_ready, tt + 1)
                if tt:
                    act.wait_ge(sh_done, tt)
                nc.scalar.activation(sh_s[:], bank[3 + tt][:, 0:F], ACT.Silu).then_inc(sh_silu, 1)
            for kk in range(KF):
                act.wait_ge(shT_ready, kk + 1)
                nc.scalar.activation(shT_hi[:, kk, :], bank[7 if kk == 0 else 2][:], ACT.Copy).then_inc(shT_hi_done, 1)
            hi_at(56, (shd_ready, 8))
            hi_at(57, (sh_ready, NT))
            hi_at(58)
            for n in range(4):
                for m in range(2):
                    k = 2 * n + m
                    act.wait_ge(ple_ready[k % 3], k // 3 + 1)
                    if k >= 2:
                        act.wait_ge(ple_done, 2 * (k - 1))
                    nc.scalar.activation(ple_s[:, m, :], bank[k % 3][:], ACT.Sigmoid).then_inc(ple_sig, 1)
                k = 2 * n + 1
                hi_at(59 + n, (ple_ready[k % 3], k // 3 + 1))

            sets_hi = (split_hi, split_hi_b)

            def expert_hi(x, s):
                slot = 3 * x.par + s
                act.wait_ge(raw_full[slot], 16 * (x.i + 1) if x.par else 16 * (x.i + 21))
                nc.scalar.activation(sets_hi[x.par][:, s, :], raw[:, slot, :], ACT.Copy).then_inc(hi_done, 1)

            def gathered_hi(x):
                act.wait_ge(xgT_ready, x.e + 1)
                for half in range(2):
                    nc.scalar.activation(xgT_hi[x.par][:, 4 * half:4 * half + 4, :].rearrange("p k n -> p (k n)"), bank[2 + half][:],
                                         ACT.Copy).then_inc(xgTh_done, 1)

            gathered_hi(Expert(0, 0))
            act.wait_ge(ple_done, 16)

            def expert_act(x, back, ahead, tables):
                if ahead:
                    expert_hi(x.next(), 0)
                if back:
                    act.wait_ge(exT_ready, x.e)
                    nc.scalar.activation(exT_hi[:].rearrange("p k n -> p (k n)"), bank[4][:, 0:KF * P], ACT.Copy).then_inc(exTh_done, 1)
                if ahead:
                    gathered_hi(x.next())
                    expert_hi(x.next(), 1)
                if ahead or x.par:
                    act.wait_ge(gu_ready, x.e + 1)
                    nc.scalar.activation(ex_h[:], bank[x.par][:, 0:F], ACT.Silu).then_inc(silu_done, 1)
                if back:
                    act.wait_ge(y_ready, x.e)
                    act.wait_ge(y_free, x.e)
                    for half in range(2):
                        nc.scalar.activation(y_out[1 - x.par][:, 512 * half:512 * (half + 1)], bank[6 + half][:], ACT.Copy).then_inc(y_done, 1)
                if ahead:
                    expert_hi(x.next(), 2)

            run_experts(act, expert_act, E)

            def over_act(e, r, n):
                for s in range(3):
                    act.wait_ge(over_loaded, 48 * n)
                    nc.scalar.activation(split_hi[:, s, :], raw[:, s, :], ACT.Copy).then_inc(over_hi, 1)
                act.wait_ge(over_turned, n)
                for half in range(2):
                    nc.scalar.activation(xgT_hi[0][:, 4 * half:4 * half + 4, :].rearrange("p k n -> p (k n)"), bank[2 + half][:],
                                         ACT.Copy).then_inc(over_xh, 1)
                act.wait_ge(over_gu, n)
                nc.scalar.activation(ex_h[:], bank[0][:, 0:F], ACT.Silu).then_inc(over_silu, 1)
                act.wait_ge(over_exT, n)
                nc.scalar.activation(exT_hi[:].rearrange("p k n -> p (k n)"), bank[4][:, 0:KF * P], ACT.Copy).then_inc(over_exh, 1)
                act.wait_ge(over_y, n)
                for half in range(2):
                    nc.scalar.activation(y_out[0][:, 512 * half:512 * (half + 1)], bank[6 + half][:], ACT.Copy).then_inc(over_copied, 1)

            further_rounds(act, over_act)
            rsqrt_act(2)

        @block.vector
        def _(dve):
            ch = Chain(dve, dve_chain)

            def lo(turn, s):
                slot = s % 3
                dve.wait_ge(hi_done, turn.piece(s) + 1)
                nc.vector.tensor_tensor(split_lo[:, slot, :], raw[:, slot, :], split_hi[:, slot, :].bitcast(F32),
                                        ALU.subtract).then_inc(lo_done, 1)

            for s_, n_ in ((ya_lo_done, 1), (mixa_done, 2), (ybl_done, 2)):
                dve.sem_inc(s_, n_)
            dve.memset(conv_u[:, :, 0:2], 0.0).then_inc(consts_made, 1)
            dve.memset(v_ext[:, :, :, DH:DH + 2], 1.0).then_inc(consts_made, 1)
            for kk in range(KD):
                dve.wait_ge(xT_hi_done, kk + 1)
                nc.vector.tensor_tensor(xT_lo[:, kk, :], bank[kk][:], xT_hi[:, kk, :].bitcast(F32), ALU.subtract).then_inc(xT_lo_done, 1)
            dve.wait_ge(wg_split, 1)
            nc.vector.tensor_tensor(wg_lo[:], wg_raw[:], wg_hi[:].bitcast(F32), ALU.subtract).then_inc(wg_split, 1)
            for s in range(3):
                lo(Turn(0, 3, 0), s)
            dve.wait_ge(gates_ready, 1)
            nc.vector.tensor_copy(gate_tok[:].rearrange("p t g -> p (t g)"), bank[2][:, 0:NT * 2 * HEADS]).then_inc(gates_used, 1)
            dve.wait_ge(gates_ready, 2)
            nc.vector.tensor_copy(params[:], bank[5][:, 0:32]).then_inc(gates_used, 1)
            i_pre, nabs, f_pre, logf, run_sum, tmp = gt[0], gt[2], gt[1], gt[3], gt[4], gt[5]
            ch.link(nc.vector.tensor_scalar(i_pre[:], bank[3][0:HEADS, :], bias_if[:, 0:1], None, ALU.add))
            ch.link(nc.vector.tensor_scalar(f_pre[:], bank[4][0:HEADS, :], bias_if[:, 1:2], None, ALU.add))
            nc.vector.scalar_tensor_tensor(nabs[:], f_pre[:], -1.0, f_pre[:], ALU.mult, ALU.max).then_inc(gate_step, 1)
            dve.wait_ge(gate_fn, 2)
            ch.link(nc.vector.scalar_tensor_tensor(logf[:], f_pre[:], 0.0, nabs[:], ALU.min, ALU.subtract))
            ch.link(nc.vector.tensor_tensor_scan(tmp[:], logf[:], logf[:], 0.0, ALU.add, ALU.bypass))
            ch.link(nc.vector.tensor_tensor(i_pre[:], i_pre[:], tmp[:], ALU.subtract))
            ch.link(nc.vector.tensor_tensor_scan(run_max[:], i_pre[:], i_pre[:], 0.0, ALU.max, ALU.bypass))
            nc.vector.tensor_tensor(run_sum[:], tmp[:], run_max[:], ALU.add).then_inc(gate_step, 1)
            dve.wait_ge(gates_ready, 3)
            nc.vector.tensor_copy(g_tok[:].rearrange("p t h -> p (t h)"), bank[6][:, 0:NT * HEADS]).then_inc(gates_used, 1)
            nc.vector.tensor_copy(guard[:].rearrange("p t h -> p (t h)"), bank[6][:, 64:64 + NT * HEADS]).then_inc(gates_used, 1)
            dve.wait_ge(gates_used, 4)
            for kk in range(KF):
                dve.wait_ge(xT_hi_done, KD + kk + 1)
                nc.vector.tensor_tensor(pT_lo[:, kk, :], bank[kk][:], pT_hi[:, kk, :].bitcast(F32), ALU.subtract).then_inc(xT_lo_done, 1)

            with dve.Fori(0, 4) as i:
                ch.enter_loop(i, 30)
                t = Turn(0, 6, i)
                h_of = lambda hl: bass.ds(2 * i + hl, 1)

                def acc(tile):
                    b, use = t.tile(tile)
                    dve.wait_ge(acc_full[b], use + 1)
                    return bank[b][:], acc_free[b]

                def select_max(hl):
                    nc.vector.tensor_scalar(max_sel[:, hl, :], run_max[:], ident[0:HEADS, h_of(hl)], None, ALU.mult).then_inc(sel_done, 1)

                def exponents(hl):
                    dve.wait_ge(mb_ready, 2 * i + hl + 1)
                    for a in range(NT):
                        nc.vector.tensor_scalar(decay[:, hl, SEG[a]:SEG[a] + SEQ - P * a], MB[:, P * a:SEQ],
                                                g_tok[:, a, h_of(hl)], 0.0, ALU.subtract, ALU.max).then_inc(arg_done, 1)

                def scores(hl):
                    dve.wait_ge(s_ready, 2 * i + hl + 1)
                    dve.wait_ge(mask_done, 8 * i + 4 * hl + 4)
                    for a in range(NT):
                        b, c0 = S_PLACE[a]
                        seg = decay[:, hl, SEG[a]:SEG[a] + SEQ - P * a]
                        nc.vector.tensor_tensor(seg, b[:, c0:c0 + SEQ - P * a], seg, ALU.mult).then_inc(pt_done, 1)

                def normalise(hl):
                    dve.wait_ge(sq_done, 8 * i + 4 * hl + 4)
                    den3 = NUM[:, 0:390].rearrange("p (j n) -> p j n", j=3)[:, :, DH]
                    for cols, den in ((slice(0, 3), den3), (slice(3, 4), S2[:, 256 + DH:257 + DH])):
                        ch.link(nc.vector.scalar_tensor_tensor(hs[:, 1, cols], den, -1.0, guard[:, cols, 2 * i + hl], ALU.mult, ALU.max))
                        ch.link(nc.vector.tensor_tensor(hs[:, 1, cols], den, hs[:, 1, cols], ALU.max))
                    ch.link(nc.vector.reciprocal(hs[:, 2, :], hs[:, 1, :]))
                    ch.link(nc.vector.tensor_tensor(hs[:, 3, :], hs[:, 2, :], hs[:, 2, :], ALU.mult))
                    ch.link(nc.vector.scalar_tensor_tensor(hs[:, 3, :], hs[:, 0, :], 1.0 / DH, hs[:, 3, :], ALU.mult, ALU.mult))
                    nc.vector.tensor_scalar(hs[:, 4, :], hs[:, 3, :], RMS_EPS, None, ALU.add).then_inc(ln_in, 1)
                    dve.wait_ge(ln_out, 4 * i + 2 * hl + 2)
                    ch.link(nc.vector.tensor_tensor(hs[:, 7, :], hs[:, 6, :], hs[:, 6, :], ALU.mult))
                    ch.link(nc.vector.tensor_tensor(hs[:, 7, :], hs[:, 7, :], hs[:, 4, :], ALU.mult))
                    ch.link(nc.vector.tensor_scalar(hs[:, 7, :], hs[:, 7, :], -0.5, 1.5, ALU.mult, ALU.add))
                    ch.link(nc.vector.tensor_tensor(hs[:, 7, :], hs[:, 7, :], hs[:, 6, :], ALU.mult))
                    ch.link(nc.vector.tensor_tensor(hs[:, 8, :], hs[:, 7, :], hs[:, 2, :], ALU.mult))
                    for j in range(NT):
                        b, c0 = NUM_PLACE[j]
                        nc.vector.tensor_scalar(head_out[:, j, :], b[:, c0:c0 + DH], hs[:, 8, j:j + 1], None, ALU.mult).then_inc(head_done, 1)

                lo(t, 3)
                lo(t, 4)
                for m in range(2):
                    src, free = acc(4 + m)
                    nc.vector.tensor_copy(v_ext[:, 2 * m:2 * m + 2, :, 0:DH], src.rearrange("p (t h d) -> p t h d", t=2, h=2)).then_inc(free, 1)
                lo(t, 5)
                select_max(0)
                select_max(1)
                exponents(0)
                lo(t, 6)
                scores(0)

                def gate_in(m):
                    src, free = acc(8 + m)
                    b, use = t.tile(6 + m)
                    dve.wait_ge(acc_free[b], use + 2)
                    nc.vector.tensor_tensor(conv_u[:, m, 2:SEQ + 2], src, conv_c[:, m, :], ALU.mult).then_inc(free, 1)

                gate_in(0)
                normalise(0)
                exponents(1)
                gate_in(1)
                lo(t, 7)

                def conv(m):
                    w = lambda j: params[:, bass.ds(8 * j + m + 2 * i, 1)]
                    if m == 0:
                        b, use = t.tile(9)
                        dve.wait_ge(acc_free[b], use + 2)
                    ch.link(nc.vector.tensor_scalar(conv_c[:, m, :], conv_u[:, m, 0:SEQ], w(0), None, ALU.mult))
                    for j in (1, 2):
                        ch.link(nc.vector.scalar_tensor_tensor(conv_c[:, m, :], conv_u[:, m, j:j + SEQ], w(j), conv_c[:, m, :], ALU.mult, ALU.add))

                def gate_out(m):
                    src, free = acc(10 + m)
                    nc.vector.tensor_tensor(conv_c[:, m, :], src, conv_c[:, m, :], ALU.mult).then_inc(free, 1)

                def ya_lo(m):
                    dve.wait_ge(ya_hi_done, 2 * i + m + 1)
                    nc.vector.tensor_tensor(yaT_lo[:, bass.ds(2 * i + m, 1), :], conv_c[:, m:m + 1, :],
                                            yaT_hi[:, bass.ds(2 * i + m, 1), :].bitcast(F32), ALU.subtract).then_inc(ya_lo_done, 1)

                conv(0)
                conv(1)
                scores(1)
                gate_out(0)
                ya_lo(0)
                normalise(1)
                gate_out(1)
                ya_lo(1)
                lo(t, 8)
                ch.leave_loop(4)

            def ready(turn, tile):
                b, use = turn.tile(tile)
                dve.wait_ge(acc_free[b], use + 2)

            dve.wait_ge(tr_done, 1 + HEADS)
            with dve.Fori(0, 4) as i:
                t = Turn(24, 3, i)
                c = lambda m: bass.ds(2 * i + m, 1)
                lo(t, 3)
                for m in range(2):
                    ready(t, 2 + m)
                    nc.vector.tensor_tensor(mixed_a[:, c(m), :], branch[:, m:m + 1, :], merge_g[:, m:m + 1, :], ALU.mult).then_inc(mixa_done, 1)
                lo(t, 4)
                for m in range(2):
                    ready(t, 4 + m)
                    nc.vector.scalar_tensor_tensor(yb_tmp[:, m:m + 1, :], hT[:, c(m), :], params[:, bass.ds(2 * i + m + 24, 1)],
                                                   yb_tmp[:, m:m + 1, :], ALU.mult, ALU.mult).then_inc(yb_done, 1)
                lo(t, 5)
                for m in range(2):
                    dve.wait_ge(ybh_done, 2 * i + m + 1)
                    nc.vector.tensor_tensor(ybT_lo[:, c(m), :], yb_tmp[:, m:m + 1, :], ybT_hi[:, c(m), :].bitcast(F32), ALU.subtract).then_inc(ybl_done, 1)

            with dve.Fori(0, 4) as i:
                t = Turn(36, 3, i)
                c = lambda m: bass.ds(2 * i + m, 1)
                lo(t, 3)
                lo(t, 4)
                for m in range(2):
                    b, use = t.tile(4 + m)
                    ready(t, 2 + m)
                    dve.wait_ge(acc_full[b], use + 1)
                    nc.vector.tensor_tensor(branch[:, m, :], bank[b][:], merge_g[:, m, :], ALU.mult).then_inc(acc_free[b], 1)
                    dve.wait_ge(acc_free[b], use + 2)
                    nc.vector.tensor_tensor(branch[:, m:m + 1, :], branch[:, m:m + 1, :], mixed_a[:, c(m), :], ALU.add).then_inc(mix_done, 1)
                for m in range(2):
                    dve.wait_ge(mixh_done, 2 * i + m + 1)
                    nc.vector.tensor_tensor(mix_lo[:, c(m), :], branch[:, m:m + 1, :], mix_hi[:, c(m), :].bitcast(F32), ALU.subtract).then_inc(mixl_done, 1)
                lo(t, 5)

            def lo_at(n, width=2048):
                dve.wait_ge(hi_done, n + 1)
                nc.vector.tensor_tensor(split_lo[:, n % 3, 0:width], raw[:, n % 3, 0:width],
                                        split_hi[:, n % 3, 0:width].bitcast(F32), ALU.subtract).then_inc(lo_done, 1)

            def moments(src, tt):
                for half in range(2):
                    ch.link(nc.vector.bn_stats(bn[:, half, :], src[:, tt, 512 * half:512 * (half + 1)]))
                ch.link(nc.vector.bn_aggr(bn_mv[:, tt, :], bn[:]))

            def rstd(k):
                nc.vector.tensor_scalar(ln_s[:, 0, :], bn_mv[:, :, 1], LN_EPS, None, ALU.add).then_inc(seed_in, 1)
                dve.wait_ge(seed_out, 2 * k)
                y0 = ln_s[:, 2, :]
                ch.link(nc.vector.tensor_tensor(ln_s[:, 3, :], y0, y0, ALU.mult))
                ch.link(nc.vector.tensor_tensor(ln_s[:, 3, :], ln_s[:, 3, :], ln_s[:, 0, :], ALU.mult))
                ch.link(nc.vector.tensor_scalar(ln_s[:, 3, :], ln_s[:, 3, :], -0.5, 1.5, ALU.mult, ALU.add))
                ch.link(nc.vector.tensor_tensor(ln_s[:, 4, :], ln_s[:, 3, :], y0, ALU.mult))

            dve.wait_ge(x1_loaded, 16)
            out_turn = Turn(48, 12, 0)
            for s in range(4):
                for m in range(2):
                    b, use = out_turn.tile(2 * s + m)
                    dve.wait_ge(acc_full[b], use + 1)
                    blk = x1[:, 2 * m:2 * m + 2, COLS * s:COLS * (s + 1)]
                    nc.vector.scalar_tensor_tensor(blk, blk, ALPHA, bank[b][:].rearrange("p (t n) -> p t n", t=2),
                                                   ALU.mult, ALU.add).then_inc(acc_free[b], 1)
                lo_at(51 + s, width=KD * E if s == 1 else 2048)
            dve.wait_ge(lo_done, 55)
            for tt in range(NT):
                moments(x1, tt)
            rstd(1)
            dve.wait_ge(ln_loaded, 32)
            for tt in range(NT):
                ch.link(nc.vector.tensor_scalar(x1[:, tt, :], x1[:, tt, :], bn_mv[:, tt, 0:1], ln_s[:, 4, tt:tt + 1], ALU.subtract, ALU.mult))
                nc.vector.tensor_tensor(x1[:, tt, :], x1[:, tt, :], ln_g[:], ALU.mult).then_inc(x1_norm, 1)
            dve.wait_ge(iota_done, 4)
            ch.link(nc.vector.tensor_copy(iota_row[:], iota_i[:]))
            ch.link(nc.vector.tensor_scalar(before[:], iota_s[:], 0, None, ALU.is_gt))
            ch.link(nc.vector.tensor_copy(tok_id[:], iota_t[:]))
            ch.link(nc.vector.tensor_tensor(lower_b[:], causal[:], ident[:], ALU.subtract))
            ch.link(nc.vector.tensor_copy(ones_b[:], ones_f[:]))
            ch.link(nc.vector.memset(slot_of[:, :, E:E + 2], -1.0))
            ch.link(nc.vector.memset(route_cols[:, :, E:E + 2, :].bitcast(F32), 0.0))
            for kk in range(KD):
                dve.wait_ge(x1T_hi_done, kk + 1)
                nc.vector.tensor_tensor(x1T_lo[:, kk, :], bank[3 + kk % 5][:], x1T_hi[:, kk, :].bitcast(F32), ALU.subtract).then_inc(x1T_lo_done, 1)
            lo_at(55)
            dve.wait_ge(scores_done, 1)
            dve.wait_ge(rb_loaded, 16)
            bc = lambda ap, shape: ap.broadcast_to(shape)
            ch.link(nc.vector.tensor_tensor(sel[:], scores_s[:], r_bias[:].rearrange("p (a e) -> p a e", a=1).broadcast_to([P, NT, E]), ALU.add))
            for tg in range(NT * 8):
                nc.vector.max(out=top_g[:, tg, :], in_=sel[:].rearrange("p t (g e) -> p (t g) e", g=8)[:, tg, :]).then_inc(dve_chain, 1)
                ch.step += 1
            dve.wait_ge(dve_chain, ch.step)
            ch.link(nc.vector.tensor_tensor(gsc[:].rearrange("p t g -> p (t g)"), top_g[:, :, 0], top_g[:, :, 1], ALU.add))
            other = gsc[:].rearrange("p t (a g) -> p t a g", a=1).broadcast_to([P, NT, 8, 8])
            own = gsc[:].rearrange("p t (g a) -> p t g a", a=1).broadcast_to([P, NT, 8, 8])
            ch.link(nc.vector.tensor_tensor(cmp_gt[:], other, own, ALU.is_gt))
            ch.link(nc.vector.tensor_tensor(cmp_eq[:], other, own, ALU.is_equal))
            ch.link(nc.vector.tensor_tensor(cmp_eq[:], cmp_eq[:], before[:].rearrange("p (a g) h -> p a g h", a=1).broadcast_to([P, NT, 8, 8]), ALU.mult))
            ch.link(nc.vector.tensor_tensor(cmp_gt[:], cmp_gt[:], cmp_eq[:], ALU.add))
            ch.link(nc.vector.tensor_reduce(gcnt[:], cmp_gt[:], AX_X, ALU.add))
            ch.link(nc.vector.tensor_scalar(gmask[:], gcnt[:], float(TOP_GROUPS), None, ALU.is_lt))
            ch.link(nc.vector.tensor_scalar(gcnt[:], gmask[:], 1.0, LOW, ALU.subtract, ALU.mult))
            by_group = lambda ap: ap.rearrange("p t (g e) -> p (t g) e", g=8)
            spread = lambda ap: ap.rearrange("p t (g a) -> p (t g) a", a=1).broadcast_to([P, NT * 8, 8])
            ch.link(nc.vector.tensor_tensor(by_group(cand[:]), by_group(sel[:]), spread(gmask[:]), ALU.mult))
            ch.link(nc.vector.tensor_tensor(by_group(cand[:]), by_group(cand[:]), spread(gcnt[:]), ALU.add))
            for tt in range(NT):
                ch.link(nc.vector.max(out=top8[:, tt, :], in_=cand[:, tt, :]))
                ch.link(nc.vector.match_replace(out=rest[:, tt, :], in_to_replace=top8[:, tt, :], in_values=cand[:, tt, :], imm_value=-2 * LOW))
            ch.link(nc.vector.tensor_scalar(chosen[:], rest[:], -2 * LOW, None, ALU.is_equal))
            nc.vector.tensor_copy(chosen_b[:], chosen[:]).then_inc(chosen_done, 1)
            ch.link(nc.vector.tensor_tensor(wsel[:], scores_s[:], chosen[:], ALU.mult))
            ch.link(nc.vector.tensor_reduce(wsum[:, 0, :], wsel[:], AX_X, ALU.add))
            ch.link(nc.vector.reciprocal(wsum[:, 1, :], wsum[:, 0, :]))
            for tt in range(NT):
                ch.link(nc.vector.tensor_scalar(wsel[:, tt, :], wsel[:, tt, :], wsum[:, 1, tt:tt + 1], ROUTED_SCALE, ALU.mult, ALU.mult))
                ch.link(nc.vector.tensor_tensor_scan(rank[:, tt, :], chosen[:, tt, :], chosen[:, tt, :], 0.0, ALU.add, ALU.bypass))
                ch.link(nc.vector.scalar_tensor_tensor(route_cols[:, tt, 0:E, 1], rank[:, tt, :], tok_id[:, 1, tt:tt + 1], chosen[:, tt, :], ALU.add, ALU.subtract))
                ch.link(nc.vector.tensor_scalar(route_cols[:, tt, 0:E, 0], chosen[:, tt, :], 0.0, tok_id[:, 0, tt:tt + 1], ALU.mult, ALU.add))
            ch.link(nc.vector.tensor_copy(route_cols[:, :, 0:E, 2], wsel[:]))
            ch.link(nc.vector.tensor_tensor(route_cols[:, :, 0:E, 3], wsel[:], route_cols[:, :, 0:E, 2].bitcast(F32), ALU.subtract))

            def tables():
                dve.wait_ge(pos_ready, 1)
                pos = bank[1][:, 0:NT * E].rearrange("p (t e) -> p t e", t=NT)
                ch.link(nc.vector.scalar_tensor_tensor(rank[:], pos, 1.0, chosen[:], ALU.add, ALU.mult))
                ch.link(nc.vector.tensor_scalar(slot_of[:, :, 0:E], rank[:], 1.0, None, ALU.subtract))
                ch.link(nc.vector.tensor_reduce(counts[:, 0:1], bank[1][:, NT * E:NT * E + E], AX_X, ALU.max))
                nc.vector.tensor_copy(counts_i[:], counts[:, 0:1]).then_inc(tables_done, 1)

            for tt in range(NT):
                dve.wait_ge(sh_silu, tt + 1)
                nc.vector.tensor_tensor(sh_h[tt][:], bank[3 + tt][:, F:2 * F], sh_s[:], ALU.mult).then_inc(sh_done, 1)
            tables()
            for kk in range(KF):
                dve.wait_ge(shT_hi_done, kk + 1)
                nc.vector.tensor_tensor(shT_lo[:, kk, :], bank[7 if kk == 0 else 2][:], shT_hi[:, kk, :].bitcast(F32), ALU.subtract).then_inc(shT_lo_done, 1)
            dve.wait_ge(y_init, NT)
            for half in range(2):
                for tt in range(NT):
                    k = NT * half + tt
                    dve.wait_ge(shd_ready, k + 1)
                    blk = y_acc[:, tt, 512 * half:512 * (half + 1)]
                    nc.vector.tensor_tensor(blk, bank[3 + tt][:], blk, ALU.add).then_inc(shd_done, 1)
            dve.wait_ge(shd_done, 8)
            lo_at(56)
            lo_at(57)
            lo_at(58)

            def one_hot_of(e):
                where = slot_of[:, :, bass.ds(e, 1)].broadcast_to([P, NT, P])
                rows = iota_row[:].rearrange("p (a n) -> p a n", a=1).broadcast_to([P, NT, P])
                nc.vector.tensor_tensor(one_hot[:], rows, where, ALU.is_equal).then_inc(hot_done, 1)

            def slot_lists(b, e, count):
                dve.wait_ge(idx_ready, count)
                nc.vector.tensor_scalar(dst_all[:, bass.ds(e, 1)], bank[5][:, 1:2], float(OOB), None, ALU.add).then_inc(lists_written, 1)
                nc.vector.tensor_reduce(gate_all[:, bass.ds(e, 1)], bank[5][:, 2:4], AX_X, ALU.add).then_inc(lists_written, 1)
                nc.vector.tensor_scalar(tok_idx[b][:], bank[5][:, 0:1], float(OOB), None, ALU.add).then_inc(idx_done, 1)

            for n in range(4):
                for m in range(2):
                    k = 2 * n + m
                    dve.wait_ge(ple_sig, k + 1)
                    s_ = ple_s[:, m, :].rearrange("p (t n) -> p t n", t=2)
                    nc.vector.tensor_tensor(s_, s_, ple_proj[:, 2 * m:2 * m + 2, COLS * n:COLS * (n + 1)], ALU.mult).then_inc(ple_done, 1)
                    dve.wait_ge(ple_done, 2 * k + 1)
                    blk = y_acc[:, 2 * m:2 * m + 2, COLS * n:COLS * (n + 1)]
                    nc.vector.tensor_tensor(blk, blk, s_, ALU.add).then_inc(ple_done, 1)
                lo_at(59 + n)
                if n < 2:
                    one_hot_of(n)
                    slot_lists(n, n, n + 1)

            sets = ((split_hi, split_lo), (split_hi_b, split_lo_b))

            def expert_lo(x, s):
                dve.wait_ge(hi_done, 60 + 3 * x.e + s + 1)
                nc.vector.tensor_tensor(sets[x.par][1][:, s, :], raw[:, 3 * x.par + s, :], sets[x.par][0][:, s, :].bitcast(F32),
                                        ALU.subtract).then_inc(lo_done, 1)

            def gathered_lo(x):
                for half in range(2):
                    part = lambda t: t[x.par][:, 4 * half:4 * half + 4, :].rearrange("p k n -> p (k n)")
                    dve.wait_ge(xgTh_done, 2 * x.e + half + 1)
                    nc.vector.tensor_tensor(part(xgT_lo), bank[2 + half][:], part(xgT_hi).bitcast(F32), ALU.subtract).then_inc(xgTl_done, 1)

            gathered_lo(Expert(0, 0))
            one_hot_of(2)

            def expert_dve(x, back, ahead, tables):
                if ahead:
                    expert_lo(x.next(), 0)
                if back:
                    dve.wait_ge(exTh_done, x.e)
                    nc.vector.tensor_tensor(exT_lo[:].rearrange("p k n -> p (k n)"), bank[4][:, 0:KF * P],
                                            exT_hi[:].rearrange("p k n -> p (k n)").bitcast(F32), ALU.subtract).then_inc(exTl_done, 1)
                if tables:
                    slot_lists(x.par, x.e + 2, x.e + 3)
                if ahead:
                    gathered_lo(x.next())
                    expert_lo(x.next(), 1)
                if back:
                    dve.wait_ge(y_free, x.e)
                    nc.vector.tensor_copy(dst_idx[1 - x.par][:], dst_all[:, bass.ds(x.e - 1, 1)]).then_inc(dst_done, 1)
                if ahead or x.par:
                    dve.wait_ge(silu_done, x.e + 1)
                    nc.vector.scalar_tensor_tensor(ex_h[:], bank[x.par][:, F:2 * F], gate_all[:, bass.ds(x.e, 1)], ex_h[:], ALU.mult, ALU.mult).then_inc(h_done, 1)
                if tables:
                    one_hot_of(x.e + 3)
                if ahead:
                    expert_lo(x.next(), 2)

            run_experts(dve, expert_dve, E)

            def over_shift(r):
                dve.wait_ge(over_done, E * (r - 1) + 1)
                nc.vector.tensor_scalar(iota_row[:], iota_row[:], float(P), None, ALU.add).then_inc(over_shifted, 1)
                dve.wait_ge(over_shifted, r)

            def over_dve(e, r, n):
                dve.wait_ge(over_done, n)
                where = slot_of[:, :, bass.ds(e, 1)].broadcast_to([P, NT, P])
                rows = iota_row[:].rearrange("p (a n) -> p a n", a=1).broadcast_to([P, NT, P])
                nc.vector.tensor_tensor(one_hot[:], rows, where, ALU.is_equal).then_inc(over_hot, 1)
                dve.wait_ge(over_lists_ready, n)
                for idx, c in ((tok_idx[0], 0), (dst_idx[0], 1)):
                    nc.vector.tensor_scalar(idx[:], bank[5][:, c:c + 1], float(OOB), None, ALU.add).then_inc(lists_written, 1)
                nc.vector.tensor_reduce(gate_all[:, E:E + 1], bank[5][:, 2:4], AX_X, ALU.add).then_inc(over_lists, 1)
                for s in range(3):
                    dve.wait_ge(over_hi, 3 * n)
                    nc.vector.tensor_tensor(split_lo[:, s, :], raw[:, s, :], split_hi[:, s, :].bitcast(F32), ALU.subtract).then_inc(over_lo, 1)
                dve.wait_ge(over_xh, 2 * n)
                for half in range(2):
                    nc.vector.tensor_tensor(xgT_lo[0][:, 4 * half:4 * half + 4, :].rearrange("p k n -> p (k n)"), bank[2 + half][:],
                                            xgT_hi[0][:, 4 * half:4 * half + 4, :].rearrange("p k n -> p (k n)").bitcast(F32), ALU.subtract).then_inc(over_xl, 1)
                dve.wait_ge(over_silu, n)
                nc.vector.scalar_tensor_tensor(ex_h[:], bank[0][:, F:2 * F], gate_all[:, E:E + 1], ex_h[:], ALU.mult, ALU.mult).then_inc(over_h, 1)
                dve.wait_ge(over_exh, n)
                nc.vector.tensor_tensor(exT_lo[:].rearrange("p k n -> p (k n)"), bank[4][:, 0:KF * P],
                                        exT_hi[:].rearrange("p k n -> p (k n)").bitcast(F32), ALU.subtract).then_inc(over_exl, 1)

            further_rounds(dve, over_dve, before=over_shift)

            for tt in range(NT):
                dve.wait_ge(part_loaded[tt], 16)
                for k in range(8):
                    ch.link(nc.vector.tensor_tensor(y_acc[:, tt, :], y_acc[:, tt, :], parts[tt % 3][:, k, :], ALU.add))
                moments(y_acc, tt)
                if tt == 0:
                    dve.sem_inc(part_done, 1)
            rstd(2)
            dve.wait_ge(ln2_loaded, 32)
            for tt in range(NT):
                ch.link(nc.vector.tensor_scalar(y_acc[:, tt, :], y_acc[:, tt, :], bn_mv[:, tt, 0:1], ln_s[:, 4, tt:tt + 1], ALU.subtract, ALU.mult))
                ch.link(nc.vector.tensor_tensor(y_acc[:, tt, :], y_acc[:, tt, :], tail_s[0][:], ALU.mult))
                nc.vector.tensor_tensor(y_acc[:, tt, :], y_acc[:, tt, :], tail_s[1][:], ALU.add).then_inc(out_done, 1)

        @block.tensor
        def _(pe):
            def product(out_, stat, mov, first, last):
                nc.tensor.matmul(out_, stat[0], mov[0], start=first, stop=False)
                nc.tensor.matmul(out_, stat[0], mov[1], start=False, stop=False)
                return nc.tensor.matmul(out_, stat[1], mov[0], start=False, stop=last)

            def claim(turn, tile):
                b, use = turn.tile(tile)
                pe.wait_ge(acc_free[b], use + 1)
                return b

            def weights_at(s, c0, n):
                return split_hi[:, s % 3, c0:c0 + n], split_lo[:, s % 3, c0:c0 + n]

            def channel_tile(turn, s, m, data, steps=KD):
                if m == 0:
                    pe.wait_ge(lo_done, turn.piece(s) + 1)
                b = claim(turn, 2 * s + m)
                for k in range(steps):
                    mm = product(bank[b][:], weights_at(s, COLS * k + P * m, P), (data[0][:, k, :], data[1][:, k, :]),
                                 k == 0, k == steps - 1)
                mm.then_inc(acc_full[b], 1)

            def token_tile(turn, s, m, data, steps=KD):
                if m == 0:
                    pe.wait_ge(lo_done, turn.piece(s) + 1)
                b = claim(turn, 2 * s + m)
                for t2 in range(2):
                    tok = slice((2 * m + t2) * P, (2 * m + t2 + 1) * P)
                    for k in range(steps):
                        mm = product(bank[b][:, COLS * t2:COLS * (t2 + 1)], (data[0][:, k, tok], data[1][:, k, tok]),
                                     weights_at(s, COLS * k, COLS), k == 0, k == steps - 1)
                mm.then_inc(acc_full[b], 1)

            xT, pT = (xT_hi, xT_lo), (pT_hi, pT_lo)
            pe.wait_ge(consts_made, 5)
            pe.wait_ge(x_loaded, 16)
            for kk in range(KD):
                for tt in range(NT):
                    mm = nc.tensor.transpose(bank[kk][:, P * tt:P * (tt + 1)],
                                             x_in[:, tt, :].rearrange("p (d k) -> p k d", k=KD)[:, kk, :], ident[:])
                mm.then_inc(xT_ready, 1)
            pe.wait_ge(xT_lo_done, KD)
            pe.wait_ge(wg_split, 2)
            for tt in range(NT):
                tok = slice(P * tt, P * (tt + 1))
                for k in range(KD):
                    mm = product(bank[2][:, 16 * tt:16 * (tt + 1)], (xT_hi[:, k, tok], xT_lo[:, k, tok]),
                                 (wg_hi[:, k, :], wg_lo[:, k, :]), k == 0, k == KD - 1)
            mm.then_inc(gates_ready, 1)
            pe.wait_ge(p_loaded, 16)
            for kk in range(KF):
                for tt in range(NT):
                    mm = nc.tensor.transpose(bank[kk][:, P * tt:P * (tt + 1)],
                                             p_in[:, tt, :].rearrange("p (d k) -> p k d", k=KF)[:, kk, :], ident[:])
                mm.then_inc(xT_ready, 1)
            pe.wait_ge(gates_used, 1)
            pe.wait_ge(small_loaded, 16 * 5)
            for tt in range(NT):
                nc.tensor.transpose(bank[3][0:HEADS, P * tt:P * (tt + 1)], gate_tok[:, tt, 0:HEADS], ident[:])
                nc.tensor.transpose(bank[4][0:HEADS, P * tt:P * (tt + 1)], gate_tok[:, tt, HEADS:2 * HEADS], ident[:])
            nc.tensor.transpose(bank[5][:, 0:32], param_rows[:], ident[0:32, 0:32]).then_inc(gates_ready, 1)
            pe.wait_ge(gate_step, 2)
            pe.wait_ge(gate_fn, 3)
            for tt in range(NT):
                nc.tensor.transpose(bank[6][:, HEADS * tt:HEADS * (tt + 1)], gt[0][:, P * tt:P * (tt + 1)], ident[0:HEADS, 0:HEADS])
                mm = nc.tensor.transpose(bank[6][:, 64 + HEADS * tt:64 + HEADS * (tt + 1)], gt[4][:, P * tt:P * (tt + 1)], ident[0:HEADS, 0:HEADS])
            mm.then_inc(gates_ready, 1)
            pe.wait_ge(gates_used, 4)
            pe.wait_ge(xT_lo_done, KD + KF)
            for b in range(3):
                pe.sem_inc(acc_free[b], 1)

            with pe.Fori(0, 4) as i:
                t = Turn(0, 6, i)

                def spread_max(hl):
                    pe.wait_ge(sel_done, 2 * i + hl + 1)
                    nc.tensor.matmul(MB[:], ones_f[0:HEADS, :], max_sel[:, hl, :], start=True, stop=True).then_inc(mb_ready, 1)

                def score_products(hl):
                    for a in range(NT):
                        b, c0 = S_PLACE[a]
                        mm = nc.tensor.matmul(b[:, c0:c0 + SEQ - P * a], kT[:, hl, P * a:P * (a + 1)],
                                              qT[:, hl, P * a:SEQ], start=True, stop=True)
                    mm.then_inc(s_ready, 1)

                def numerators(hl):
                    pe.wait_ge(pt_done, 8 * i + 4 * hl + 4)
                    for j in range(NT):
                        b, c0 = NUM_PLACE[j]
                        for a in range(j + 1):
                            c = SEG[a] + P * (j - a)
                            mm = nc.tensor.matmul(b[:, c0:c0 + DH + 2], decay[:, hl, c:c + P], v_ext[:, a, hl, :],
                                                  start=(a == 0), stop=(a == j))
                    mm.then_inc(num_ready, 1)

                def turn_head(hl):
                    pe.wait_ge(head_done, 8 * i + 4 * hl + 4)
                    for j in range(NT):
                        mm = nc.tensor.transpose(MB[:, P * j:P * (j + 1)], head_out[:, j, :], ident[:])
                    mm.then_inc(tr_ready, 1)

                for s in range(2):
                    for m in range(2):
                        channel_tile(t, s, m, xT)
                for m in range(2):
                    token_tile(t, 2, m, xT)
                channel_tile(t, 3, 0, xT)
                pe.wait_ge(acc_free[0], t.tile(3)[1] + 2)
                pe.wait_ge(tr_done, 2 * i + 1)
                spread_max(0)
                score_products(0)
                channel_tile(t, 3, 1, xT)
                channel_tile(t, 4, 0, xT)
                numerators(0)
                pe.wait_ge(arg_done, 8 * i + 4)
                spread_max(1)
                channel_tile(t, 4, 1, xT)
                pe.wait_ge(head_done, 8 * i + 4)
                score_products(1)
                pe.wait_ge(arg_done, 8 * i + 8)
                turn_head(0)
                channel_tile(t, 5, 0, xT)
                numerators(1)
                channel_tile(t, 5, 1, xT)
                pe.wait_ge(tr_done, 2 * i + 2)
                turn_head(1)

            yaT, ybT = (yaT_hi, yaT_lo), (ybT_hi, ybT_lo)
            pe.wait_ge(ya_lo_done, 1 + KD)
            with pe.Fori(0, 4) as i:
                t = Turn(24, 3, i)
                for s, data in enumerate([yaT, xT, xT]):
                    for m in range(2):
                        channel_tile(t, s, m, data)
            with pe.Fori(0, 4) as i:
                t = Turn(36, 3, i)
                for m in range(2):
                    token_tile(t, 0, m, pT, steps=KF)
                for m in range(2):
                    channel_tile(t, 1, m, xT)
                pe.wait_ge(ybl_done, 2 + KD)
                for m in range(2):
                    channel_tile(t, 2, m, ybT)

            mixT, x1T = (mix_hi, mix_lo), (x1T_hi, x1T_lo)
            pe.wait_ge(mixl_done, KD)
            out_turn = Turn(48, 12, 0)
            for s in range(4):
                for m in range(2):
                    token_tile(out_turn, s, m, mixT)
            pe.wait_ge(x1_done, NT)
            for kk in range(KD):
                if kk >= 5:
                    pe.wait_ge(x1T_lo_done, kk - 4)
                for tt in range(NT):
                    mm = nc.tensor.transpose(bank[3 + kk % 5][:, P * tt:P * (tt + 1)],
                                             x1[:, tt, :].rearrange("p (d k) -> p k d", k=KD)[:, kk, :], ident[:])
                mm.then_inc(x1T_ready, 1)
            for b in range(3):
                pe.wait_ge(acc_free[b], 1 + (104 - b + 2) // 3)
            pe.wait_ge(lo_done, 53)
            pe.wait_ge(x1T_lo_done, KD)
            for tt in range(NT):
                tok = slice(P * tt, P * (tt + 1))
                for k in range(KD):
                    mm = product(bank[0][:, E * tt:E * (tt + 1)], (x1T_hi[:, k, tok], x1T_lo[:, k, tok]),
                                 weights_at(52, E * k, E), k == 0, k == KD - 1)
            mm.then_inc(router_ready, 1)
            pe.wait_ge(lo_done, 56)
            for tt in range(NT):
                tok = slice(P * tt, P * (tt + 1))
                for k in range(KD):
                    mm = product(bank[3 + tt][:], (x1T_hi[:, k, tok], x1T_lo[:, k, tok]),
                                 (split_hi[:, 0:2, F * k:F * (k + 1)], split_lo[:, 0:2, F * k:F * (k + 1)]), k == 0, k == KD - 1)
                mm.then_inc(sh_ready, 1)
            pe.wait_ge(chosen_done, 1)
            for tt in range(NT):
                for t2 in range(tt + 1):
                    nc.tensor.matmul(bank[1][:, E * tt:E * (tt + 1)], ones_b[:] if t2 < tt else lower_b[:], chosen_b[:, t2, :],
                                     start=(t2 == 0), stop=(t2 == tt))
            for t2 in range(NT):
                mm = nc.tensor.matmul(bank[1][:, NT * E:(NT + 1) * E], ones_b[:], chosen_b[:, t2, :], start=(t2 == 0), stop=(t2 == NT - 1))
            mm.then_inc(pos_ready, 1)
            for kk in range(KF):
                for tt in range(NT):
                    if kk == 0:
                        pe.wait_ge(sh_done, tt + 1)
                    mm = nc.tensor.transpose(bank[7 if kk == 0 else 2][:, P * tt:P * (tt + 1)],
                                             sh_h[tt][:].rearrange("p (d k) -> p k d", k=KF)[:, kk, :], ident[:])
                mm.then_inc(shT_ready, 1)
            pe.wait_ge(shT_lo_done, KF)
            for half in range(2):
                for tt in range(NT):
                    if half:
                        pe.wait_ge(shd_done, tt + 1)
                    tok = slice(P * tt, P * (tt + 1))
                    for k in range(KF):
                        mm = product(bank[3 + tt][:], (shT_hi[:, k, tok], shT_lo[:, k, tok]),
                                     weights_at(53, D * k + 512 * half, 512), k == 0, k == KF - 1)
                    mm.then_inc(shd_ready, 1)

            def slot_products(e, count):
                pe.wait_ge(hot_done, count)
                for tt in range(NT):
                    mm = nc.tensor.matmul(bank[5][:, 0:4], one_hot[:, tt, :], route_cols[:, tt, bass.ds(e, 1), :].rearrange("p a c -> p (a c)"),
                                          start=(tt == 0), stop=(tt == NT - 1))
                mm.then_inc(idx_ready, 1)

            def turn_rows(x):
                pe.wait_ge((gathered0, gathered1)[x.par], 16 * (x.i + 1))
                for k in range(KD):
                    mm = nc.tensor.transpose(bank[2 + k // 4][:, P * (k % 4):P * (k % 4 + 1)],
                                             xg[x.par][:].rearrange("p (d k) -> p k d", k=KD)[:, k, :], ident[:])
                mm.then_inc(xgT_ready, 1)

            pe.wait_ge(tables_done, 1)
            for n in range(4):
                pe.wait_ge(lo_done, 57 + n)
                for m in range(2):
                    k = 2 * n + m
                    if k >= 3:
                        pe.wait_ge(ple_sig, k - 2)
                    for t2 in range(2):
                        tok = slice((2 * m + t2) * P, (2 * m + t2 + 1) * P)
                        for kk in range(KD):
                            mm = product(bank[k % 3][:, COLS * t2:COLS * (t2 + 1)], (x1T_hi[:, kk, tok], x1T_lo[:, kk, tok]),
                                         weights_at(56 + n, COLS * kk, COLS), kk == 0, kk == KD - 1)
                    mm.then_inc(ple_ready[k % 3], 1)
                if n in (1, 2):
                    if n == 1:
                        pe.wait_ge(shd_done, 8)
                    slot_products(n - 1, n)
            pe.wait_ge(ple_sig, 8)
            turn_rows(Expert(0, 0))

            sets = ((split_hi, split_lo), (split_hi_b, split_lo_b))

            def expert_pe(x, back, ahead, tables):
                def gate_up(first, end):
                    whi, wlo = sets[x.par]
                    for k in range(first, end):
                        mm = product(bank[x.par][:], (xgT_hi[x.par][:, k, :], xgT_lo[x.par][:, k, :]),
                                     (whi[:, 0:2, F * k:F * (k + 1)], wlo[:, 0:2, F * k:F * (k + 1)]), k == 0, k == KD - 1)
                    return mm

                this = ahead or x.par
                if this:
                    pe.wait_ge(lo_done, 60 + 3 * x.e + 2)
                    pe.wait_ge(xgTl_done, 2 * x.e + 2)
                    gate_up(0, KD // 2)
                if tables:
                    slot_products(x.e + 2, x.e + 3)
                if back:
                    pe.wait_ge(h_done, x.e)
                    for k in range(KF):
                        mm = nc.tensor.transpose(bank[4][:, P * k:P * (k + 1)], ex_h[:].rearrange("p (d k) -> p k d", k=KF)[:, k, :], ident[:])
                    mm.then_inc(exT_ready, 1)
                if ahead:
                    turn_rows(x.next())
                if this:
                    gate_up(KD // 2, KD).then_inc(gu_ready, 1)
                if back:
                    whi, wlo = sets[1 - x.par]
                    pe.wait_ge(exTl_done, x.e)
                    pe.wait_ge(lo_done, 60 + 3 * x.e)
                    pe.wait_ge(y_done, 2 * x.e - 1)
                    for half in range(2):
                        for k in range(KF):
                            mm = product(bank[6 + half][:], (exT_hi[:, k, :], exT_lo[:, k, :]),
                                         (whi[:, 2, D * k + 512 * half:D * k + 512 * (half + 1)],
                                          wlo[:, 2, D * k + 512 * half:D * k + 512 * (half + 1)]), k == 0, k == KF - 1)
                    mm.then_inc(y_ready, 1)

            run_experts(pe, expert_pe, E)

            def over_pe(e, r, n):
                pe.wait_ge(over_hot, n)
                for tt in range(NT):
                    mm = nc.tensor.matmul(bank[5][:, 0:4], one_hot[:, tt, :], route_cols[:, tt, bass.ds(e, 1), :].rearrange("p a c -> p (a c)"),
                                          start=(tt == 0), stop=(tt == NT - 1))
                mm.then_inc(over_lists_ready, 1)
                pe.wait_ge(over_gathered, 16 * n)
                for k in range(KD):
                    mm = nc.tensor.transpose(bank[2 + k // 4][:, P * (k % 4):P * (k % 4 + 1)],
                                             xg[0][:].rearrange("p (d k) -> p k d", k=KD)[:, k, :], ident[:])
                mm.then_inc(over_turned, 1)
                pe.wait_ge(over_lo, 3 * n)
                pe.wait_ge(over_xl, 2 * n)
                for k in range(KD):
                    mm = product(bank[0][:], (xgT_hi[0][:, k, :], xgT_lo[0][:, k, :]),
                                 (split_hi[:, 0:2, F * k:F * (k + 1)], split_lo[:, 0:2, F * k:F * (k + 1)]), k == 0, k == KD - 1)
                mm.then_inc(over_gu, 1)
                pe.wait_ge(over_h, n)
                for k in range(KF):
                    mm = nc.tensor.transpose(bank[4][:, P * k:P * (k + 1)], ex_h[:].rearrange("p (d k) -> p k d", k=KF)[:, k, :], ident[:])
                mm.then_inc(over_exT, 1)
                pe.wait_ge(over_exl, n)
                for half in range(2):
                    for k in range(KF):
                        mm = product(bank[6 + half][:], (exT_hi[:, k, :], exT_lo[:, k, :]),
                                     (split_hi[:, 2, D * k + 512 * half:D * k + 512 * (half + 1)],
                                      split_lo[:, 2, D * k + 512 * half:D * k + 512 * (half + 1)]), k == 0, k == KF - 1)
                mm.then_inc(over_y, 1)

            further_rounds(pe, over_pe)


_INS = ['x', 'p', 'w_in', 'conv_w', 'b_igate', 'b_fgate', 'mlstm_norm_g', 'w_branch_a', 'w_branch_b', 'w_out',
        'ln1_g', 'ln1_b', 'w_router', 'router_bias', 'w_exp_gate', 'w_exp_up', 'w_exp_down', 'w_sh_gate',
        'w_sh_up', 'w_sh_down', 'w_ple_gate', 'w_ple_proj', 'ln2_g', 'ln2_b']


def kernel(**inputs):
    import numpy as _np
    import concourse.bacc as _bacc
    from concourse import mybir as _mybir
    from concourse.bass_utils import run_bass_kernel_spmd as _run

    nc = _bacc.Bacc("TRN2", target_bir_lowering=False, num_devices=1)
    arrays, args = {}, []
    for name in _INS:
        a = _np.ascontiguousarray(inputs[name])
        arrays[f"in_{name}_dram"] = a
        args.append(nc.dram_tensor(f"in_{name}_dram", a.shape, _mybir.dt.from_np(a.dtype), kind="ExternalInput").ap())
    shape = inputs["x"].shape
    args.append(nc.dram_tensor("out_dram", shape, _mybir.dt.float32, kind="ExternalOutput").ap())
    hybrid_layer(nc, *args)
    r = _run(nc, [arrays], core_ids=[0])
    return r.results[0]["out_dram"]
```

```python
from contextlib import ExitStack

import concourse.bass as bass
from concourse import mybir

F32 = mybir.dt.float32
F32R = mybir.dt.float32r
I32 = mybir.dt.int32
BF16 = mybir.dt.bfloat16
ALU = mybir.AluOpType
ACT = mybir.ActivationFunctionType
AX_X = mybir.AxisListType.X

P = 128
KB = 1024


class Chain:

    def __init__(self, eng, sem):
        self.eng, self.sem, self.base, self.step = eng, sem, 0, 0

    def link(self, ins):
        ins.then_inc(self.sem, 1)
        self.step += 1
        self.eng.wait_ge(self.sem, self.base + self.step)

    def add(self, ins):
        ins.then_inc(self.sem, 1)
        self.step += 1

    def settle(self):
        self.eng.wait_ge(self.sem, self.base + self.step)

    def enter_loop(self, i, per_turn):
        self.start, self.per_turn = self.step, per_turn
        self.base = per_turn * i

    def leave_loop(self, turns):
        assert self.step - self.start == self.per_turn, (self.step - self.start, self.per_turn)
        self.base, self.step = 0, self.start + turns * self.per_turn


class Turn:

    def __init__(self, n0, k, i):
        assert n0 % 3 == 0 and k % 3 == 0
        self.n0, self.k, self.i = n0, k, i

    def piece(self, s):
        return self.n0 + self.k * self.i + s

    def third(self, s):
        return self.n0 // 3 + (self.k // 3) * self.i + s // 3

    def tile(self, t):
        return t % 3, 2 * self.n0 // 3 + (2 * self.k // 3) * self.i + t // 3


class Expert:

    def __init__(self, i, par):
        self.i, self.par = i, par
        self.e = 2 * i + par

    def next(self):
        return Expert(self.i + self.par, 1 - self.par)


def run_experts(eng, step, count):
    step(Expert(0, 0), False, True, True)
    step(Expert(0, 1), True, True, True)
    step(Expert(1, 0), True, True, True)
    with eng.Fori(1, count // 2 - 2) as i:
        step(Expert(i, 1), True, True, True)
        step(Expert(i + 1, 0), True, True, True)
    step(Expert(count // 2 - 2, 1), True, True, True)
    step(Expert(count // 2 - 1, 0), True, True, False)
    step(Expert(count // 2 - 1, 1), True, False, False)
    step(Expert(count // 2, 0), True, False, False)


def hybrid_layer(nc, x, p, w_in, conv_w, b_igate, b_fgate, norm_g, w_a, w_b, w_out, ln1_g, ln1_b,
                 w_router, router_bias, w_eg, w_eu, w_ed, w_sg, w_su, w_sd, w_pg, w_pp, ln2_g, ln2_b, out):
    _, SEQ, D = x.shape
    HEADS = b_igate.shape[1]
    DH = norm_g.shape[1] // HEADS
    PLE = p.shape[3]
    E = w_eg.shape[1]
    F = w_eg.shape[3]
    NT = SEQ // P
    KD = D // P
    KF = F // P
    ALPHA = 2.0 ** 0.25
    TOP_GROUPS, ROUTED_SCALE = 4, 2.5
    OOB = 2 * SEQ
    LOW = 1e30
    QK_SCALE = float(DH) ** -0.5
    RMS_EPS, LN_EPS = 1e-6, 1e-5
    assert SEQ == 512 and D == 1024 and DH == P and HEADS == KD and PLE == F == 256 and NT == 4

    COLS = 256
    COL = {n: j * 1024 for j, n in enumerate(["c_in", "c_out", "c_val", "q", "k", "v", "o"])}
    GATES = 7 * 1024
    MERGE = GATES + 2 * HEADS
    SEG = [0, 512, 896, 1152]
    SEGW = 1280

    x_tok = x[0].rearrange("(t p) d -> p t d", p=P)
    p_tok = p[0, 0].rearrange("(t p) d -> p t d", p=P)

    def by_row(w):
        return w.rearrange("(p k) n -> p k n", p=P)

    def by_tile(w):
        return w.rearrange("(k p) n -> p k n", p=P)

    win_r = by_row(w_in[0])
    wa_t, wb_t, wo_t = by_tile(w_a[0]), by_tile(w_b[0]), by_tile(w_out[0])
    wpp_r = by_row(w_pp[0])

    with ExitStack() as ctx:
        def sem(name):
            return ctx.enter_context(nc.semaphore(name))

        base = (nc.sbuf_base + 63) // 64 * 64

        def at(name, kb, shape, dt=F32):
            return nc.alloc_sbuf_tensor_at(name, shape, dt, offset=base + int(kb * KB))

        split_hi = at("split_hi", 0, [P, 3, 2048], F32R)
        split_lo = at("split_lo", 24, [P, 3, 2048], F32R)
        raw = at("raw", 48, [P, 6, 2048])
        decay = at("decay", 72, [P, 2, SEGW])
        head_out = at("head_out", 82, [P, NT, DH])
        conv_u = at("conv_u", 84, [P, 2, SEQ + 2])
        conv_c = at("conv_c", 88.5, [P, 2, SEQ])
        mixed_a = at("mixed_a", 72, [P, KD, SEQ])
        branch = at("branch", 88, [P, 2, SEQ])
        merge_g = at("merge_g", 92, [P, 2, SEQ])
        R = 96
        xT_hi = at("xT_hi", R, [P, KD, SEQ], F32R)
        xT_lo = at("xT_lo", R + 16, [P, KD, SEQ], F32R)
        yaT_hi = at("yaT_hi", R + 32, [P, KD, SEQ], F32R)
        yaT_lo = at("yaT_lo", R + 48, [P, KD, SEQ], F32R)
        hT = at("hT", R + 64, [P, HEADS, SEQ])
        ybT_hi = at("ybT_hi", R + 64, [P, KD, SEQ], F32R)
        ybT_lo = at("ybT_lo", R + 80, [P, KD, SEQ], F32R)
        qT = at("qT", R + 80, [P, 2, SEQ])
        kT = at("kT", R + 84, [P, 2, SEQ])
        v_ext = at("v_ext", R + 88, [P, NT, 2, DH + 2])
        run_max = at("run_max", R + 93, [HEADS, SEQ])
        pT_hi = at("pT_hi", R + 96, [P, KF, SEQ], F32R)
        pT_lo = at("pT_lo", R + 100, [P, KF, SEQ], F32R)
        max_sel = at("max_sel", R + 104, [HEADS, 2, SEQ])
        yb_tmp = at("yb_tmp", R + 104, [P, 2, SEQ])
        C = R + 108
        ident = at("ident", C, [P, P])
        causal = at("causal", C + 0.5, [P, P])
        ones_f = at("ones_f", C + 1, [P, P])
        params = at("params", C + 1.5, [P, 32])
        g_tok = at("g_tok", C + 1.625, [P, NT, HEADS])
        guard = at("guard", C + 1.75, [P, NT, HEADS])
        hs = at("hs", C + 1.875, [P, 10, NT])
        bias_if = at("bias_if", C + 2.125, [HEADS, 2])
        one_col = at("one_col", C + 2.1875, [P, 1])
        x_in = at("x_in", R + 32, [P, NT, D])
        p_in = at("p_in", R + 48, [P, NT, PLE])
        gt = [at(f"gate_tmp{j}", R + 52 + 2 * j, [HEADS, SEQ]) for j in range(6)]
        wg_raw = at("wg_raw", R + 64, [P, KD, 2 * HEADS])
        wg_hi = at("wg_hi", R + 65, [P, KD, 2 * HEADS], F32R)
        wg_lo = at("wg_lo", R + 66, [P, KD, 2 * HEADS], F32R)
        param_rows = at("param_rows", R + 68, [32, P])
        ple_proj = at("ple_proj", R + 32, [P, NT, D])
        mix_hi = at("mix_hi", R + 48, [P, KD, SEQ], F32R)
        mix_lo = at("mix_lo", 72, [P, KD, SEQ], F32R)

        x1 = at("x1", R, [P, NT, D])
        y_acc = at("y_acc", R + 16, [P, NT, D])
        ln_g = at("ln_g", 88, [P, D])
        ln_b = at("ln_b", 92, [P, D])
        x1T_hi = at("x1T_hi", R + 64, [P, KD, SEQ], F32R)
        x1T_lo = at("x1T_lo", R + 80, [P, KD, SEQ], F32R)
        T = R + 48
        scores_s = at("scores_s", T, [P, NT, E])
        sel = at("sel", T + 1, [P, NT, E])
        top_g = at("top_g", T + 2, [P, NT * 8, 8])
        cmp_gt = at("cmp_gt", T + 3, [P, NT, 8, 8])
        cmp_eq = at("cmp_eq", T + 4, [P, NT, 8, 8])
        before = at("before", R + 104.25, [P, 8, 8])
        r_bias = at("r_bias", R + 104, [P, E])
        gsc = at("gsc", T + 5.5, [P, NT, 8])
        gcnt = at("gcnt", T + 5.625, [P, NT, 8])
        gmask = at("gmask", T + 5.75, [P, NT, 8])
        top8 = at("top8", T + 5.875, [P, NT, 8])
        cand = at("cand", T + 6, [P, NT, E])
        rest = at("rest", T + 7, [P, NT, E])
        chosen = at("chosen", T + 8, [P, NT, E])
        chosen_b = at("chosen_b", T + 9, [P, NT, E], BF16)
        wsel = at("wsel", T + 10, [P, NT, E])
        slot_1 = at("slot_1", T + 11, [P, NT, E])
        wsum = at("wsum", T + 12, [P, 2, NT])
        sh_s = at("sh_s", T + 12.25, [P, F])
        sh_h = [at(f"sh_h{j}", 76 + j, [P, F]) for j in range(4)]
        shT_hi = at("shT_hi", 84, [P, KF, SEQ], F32R)
        shT_lo = at("shT_lo", 80, [P, KF, SEQ], F32R)
        ple_s = at("ple_s", R + 104, [P, 2, 512])
        router_hi = at("router_hi", R + 101.3125, [P, KD * E], F32R)
        router_lo = at("router_lo", R + 105, [P, KD * E], F32R)
        logits_t = at("logits_t", T + 13.5, [E, SEQ])
        bn_parts = at("bn_parts", R + 107.25, [P, NT, 4, 6])
        route_cols = at("route_cols", R + 96, [P, NT, E + 2, 4], F32R)
        slot_of = at("slot_of", R + 100.25, [P, NT, E + 2])
        one_hot = at("one_hot", R + 101.3125, [P, NT, P], F32R)
        ex_h = at("ex_h", R + 104, [P, F])
        exT_hi = at("exT_hi", R + 105, [P, KF, P], F32R)
        exT_lo = at("exT_lo", R + 106, [P, KF, P], F32R)
        split_hi_b = at("split_hi_b", R + 32, [P, 3, 2048], F32R)
        split_lo_b = at("split_lo_b", R + 56, [P, 3, 2048], F32R)
        xg = [at(f"xg{b}", R + 4 * b, [P, D]) for b in range(2)]
        xgT_hi = [at(f"xgT_hi{b}", R + 8 + 80 * b, [P, KD, P], F32R) for b in range(2)]
        xgT_lo = [at(f"xgT_lo{b}", R + 12 + 80 * b, [P, KD, P], F32R) for b in range(2)]
        y_out = [at(f"y_out{b}", R + 80 + 4 * b, [P, D]) for b in range(2)]
        iota_row = at("iota_row", C + 2.25, [P, P])
        lower_b = at("lower_b", C + 2.75, [P, P], BF16)
        ones_b = at("ones_b", C + 3, [P, P], BF16)
        o = C + 3.25
        tok_id = at("tok_id", o, [P, NT])
        tok_idx = [at(f"tok_idx{b}", o + 0.0625 * (1 + b), [P, 1], I32) for b in range(2)]
        dst_idx = [at(f"dst_idx{b}", o + 0.0625 * (3 + b), [P, 1], I32) for b in range(2)]
        ln_s = at("ln_s", C + 3.5625, [P, 8, NT])
        counts = at("counts", C + 3.6875, [P, 2])
        counts_i = at("counts_i", C + 3.71875, [P, 1], I32)
        bn = at("bn", C + 3.75, [P, 2, 6])
        bn_mv = at("bn_mv", C + 3.8125, [P, NT, 2])
        dst_all = at("dst_all", R + 103.3125, [P, E + 2])
        gate_all = at("gate_all", R + 103.59375, [P, E + 2])
        iota_i = at("iota_i", R + 80, [P, P], I32)
        iota_s = at("iota_s", R + 81, [P, 8, 8], I32)
        iota_t = at("iota_t", R + 82, [P, NT], I32)
        tail_s = [at(f"tail_s{j}", R + 32 + 4 * j, [P, D]) for j in range(4)]
        x1_dram = nc.dram_tensor("x1_rows", (SEQ, D), F32, kind="Internal").ap()
        y_dram = nc.dram_tensor("y_rows", (SEQ, D), F32, kind="Internal").ap()

        bank = [ctx.enter_context(nc.psum_tensor(f"bank{i}", [P, 512], F32)) for i in range(8)]
        MB, S0, S13, S2, NUM = bank[6], bank[3], bank[4], bank[5], bank[7]
        S_PLACE = [(S0, 0), (S13, 0), (S2, 0), (S13, 384)]
        NUM_PLACE = [(NUM, 0), (NUM, 130), (NUM, 260), (S2, 256)]

        consts_made = sem("consts_made")
        x_loaded = [sem(f"x_loaded{tt}") for tt in range(NT)]
        p_loaded = sem("p_loaded")
        small_loaded = sem("small_loaded")
        raw_full = [sem(f"raw_full{j}") for j in range(6)]
        hi_done = sem("hi_done")
        lo_done = sem("lo_done")
        acc_full = [sem(f"acc_full{j}") for j in range(3)]
        acc_free = [sem(f"acc_free{j}") for j in range(3)]
        xT_ready = sem("xT_ready")
        xT_hi_done = sem("xT_hi_done")
        xT_lo_done = sem("xT_lo_done")
        wg_split = sem("wg_split")
        gates_ready = sem("gates_ready")
        gates_used = sem("gates_used")
        gate_fn = sem("gate_fn")
        gate_step = sem("gate_step")
        dve_chain = sem("dve_chain")
        pool_chain = sem("pool_chain")
        sel_done = sem("sel_done")
        mb_ready = sem("mb_ready")
        arg_done = sem("arg_done")
        exp_done = sem("exp_done")
        mask_done = sem("mask_done")
        s_ready = sem("s_ready")
        pt_done = sem("pt_done")
        num_ready = sem("num_ready")
        sq_done = sem("sq_done")
        ln_in = sem("ln_in")
        ln_out = sem("ln_out")
        head_done = sem("head_done")
        tr_ready = sem("tr_ready")
        tr_done = sem("tr_done")
        ya_hi_done = sem("ya_hi_done")
        ya_lo_done = sem("ya_lo_done")
        mixa_done = sem("mixa_done")
        yb_done = sem("yb_done")
        ybh_done = sem("ybh_done")
        ybl_done = sem("ybl_done")
        mix_done = sem("mix_done")
        mixh_done = sem("mixh_done")
        mixl_done = sem("mixl_done")
        loads_issued = sem("loads_issued")
        rounds_over = sem("rounds_over")
        over_done = sem("over_done")
        over_loaded = sem("over_loaded")
        over_hi = sem("over_hi")
        over_lo = sem("over_lo")
        over_hot = sem("over_hot")
        over_lists_ready = sem("over_lists_ready")
        over_lists = sem("over_lists")
        over_shifted = sem("over_shifted")
        over_gathered = sem("over_gathered")
        over_turned = sem("over_turned")
        over_xh = sem("over_xh")
        over_xl = sem("over_xl")
        over_gu = sem("over_gu")
        over_silu = sem("over_silu")
        over_h = sem("over_h")
        over_exT = sem("over_exT")
        over_exh = sem("over_exh")
        over_exl = sem("over_exl")
        over_y = sem("over_y")
        over_copied = sem("over_copied")
        over_scattered = sem("over_scattered")
        ple_ready = [sem(f"ple_ready{j}") for j in range(3)]
        y_loaded = [sem(f"y_loaded{tt}") for tt in range(NT)]
        y_stored = sem("y_stored")
        y_free = sem("y_free")
        lists_written = sem("lists_written")
        ln_loaded = sem("ln_loaded")
        x1_loaded = sem("x1_loaded")
        rb_loaded = sem("rb_loaded")
        ln2_loaded = sem("ln2_loaded")
        x1_stored = sem("x1_stored")
        out_stored = sem("out_stored")
        seed_in = sem("seed_in")
        seed_out = sem("seed_out")
        x1_done = [sem(f"x1_done{tt}") for tt in range(NT)]
        x1_scaled = sem("x1_scaled")
        y_scaled = sem("y_scaled")
        moments_done = sem("moments_done")
        x1T_ready = sem("x1T_ready")
        x1T_hi_done = sem("x1T_hi_done")
        x1T_lo_done = sem("x1T_lo_done")
        y_init = sem("y_init")
        router_ready = sem("router_ready")
        scores_done = sem("scores_done")
        chosen_done = sem("chosen_done")
        pos_ready = sem("pos_ready")
        sh_ready = sem("sh_ready")
        sh_silu = sem("sh_silu")
        sh_done = sem("sh_done")
        shT_ready = sem("shT_ready")
        shT_hi_done = sem("shT_hi_done")
        shT_lo_done = sem("shT_lo_done")
        shd_ready = sem("shd_ready")
        shd_done = sem("shd_done")
        ple_sig = sem("ple_sig")
        ple_done = sem("ple_done")
        tables_done = sem("tables_done")
        hot_done = sem("hot_done")
        idx_ready = sem("idx_ready")
        idx_done = sem("idx_done")
        dst_done = sem("dst_done")
        gathered0 = sem("gathered0")
        gathered1 = sem("gathered1")
        scattered0 = sem("scattered0")
        scattered1 = sem("scattered1")
        xgT_ready = sem("xgT_ready")
        xgTh_done = sem("xgTh_done")
        xgTl_done = sem("xgTl_done")
        gu_ready = sem("gu_ready")
        silu_done = sem("silu_done")
        h_done = sem("h_done")
        exT_ready = sem("exT_ready")
        exTh_done = sem("exTh_done")
        exTl_done = sem("exTl_done")
        y_ready = sem("y_ready")
        y_done = sem("y_done")
        pool_tick = sem("pool_tick")
        iota_done = sem("iota_done")
        xg_clear = sem("xg_clear")
        out_done = [sem(f"out_done{tt}") for tt in range(NT)]

        def further_rounds(eng, block_of, before=None):
            eng.wait_ge(tables_done, 1)
            load_max = eng.value_load(counts_i[0:1, 0:1], min_val=0, max_val=SEQ)
            for r in range(1, NT):
                with eng.If(load_max > P * r):
                    if before:
                        before(r)
                    with eng.Fori(0, E) as e:
                        block_of(e, r, e + (E * (r - 1) + 1))

        block = ctx.enter_context(nc.Block())

        @block.sync
        def _(sp):
            for tt in range(NT):
                sp.dma_start(x_in[:, tt, :], x_tok[:, tt, :]).then_inc(x_loaded[tt], 16)
            sp.dma_start(wg_raw[:], win_r[:, :, GATES:GATES + 2 * HEADS]).then_inc(small_loaded, 16)
            sp.dma_start(param_rows[0:24, :], conv_w[0].rearrange("j (m c) -> (j m) c", c=P)).then_inc(small_loaded, 16)
            sp.dma_start(param_rows[24:32, :], norm_g[0].rearrange("(m c) -> m c", c=P)).then_inc(small_loaded, 16)
            sp.dma_start(bias_if[:, 0:1], b_igate[0].rearrange("(h a) -> h a", a=1)).then_inc(small_loaded, 16)
            sp.dma_start(bias_if[:, 1:2], b_fgate[0].rearrange("(h a) -> h a", a=1)).then_inc(small_loaded, 16)

            def load(turn, s, src, cols=None, slots=3):
                n = turn.piece(s)
                slot = s % 3
                if not isinstance(n, int):
                    sp.wait_ge(lo_done, n - 2)
                    sp.sem_inc(loads_issued, 1)
                elif n >= 3:
                    sp.wait_ge(lo_done, n - 2)
                dst = raw[:, slot, 0:src.shape[1] * src.shape[2]].rearrange("p (k n) -> p k n", k=src.shape[1])
                sp.dma_start(dst, src).then_inc(raw_full[slot], 16)

            def cols_of(w, first, i):
                return w[:, :, bass.ds(first + COLS * i, COLS)]

            def load_a(i):
                t = Turn(0, 6, i)
                for s, name in enumerate(["q", "k", "v", "c_in", "c_val", "c_out"]):
                    if isinstance(i, int) and s == 3:
                        sp.dma_start(p_in[:], p_tok).then_inc(p_loaded, 16)
                    load(t, s, cols_of(win_r, COL[name], i))

            load_a(0)
            with sp.Fori(1, 4) as i:
                load_a(i)
            with sp.Fori(0, 4) as i:
                t = Turn(24, 3, i)
                load(t, 0, cols_of(wa_t, 0, i))
                load(t, 1, cols_of(win_r, MERGE, i))
                load(t, 2, cols_of(win_r, COL["o"], i))
            with sp.Fori(0, 4) as i:
                t = Turn(36, 3, i)
                load(t, 0, cols_of(wpp_r, 0, i))
                load(t, 1, cols_of(win_r, MERGE + D, i))
                load(t, 2, cols_of(wb_t, 0, i))
            w_out_piece = lambda n: wo_t[:, :, COLS * n:COLS * (n + 1)]

            def load_at(n, src, slot):
                if n >= 3:
                    sp.wait_ge(lo_done, n - 2)
                dst = raw[:, slot, 0:src.shape[1] * src.shape[2]].rearrange("p (k n) -> p k n", k=src.shape[1])
                sp.dma_start(dst, src).then_inc(raw_full[slot], 16)

            for n in range(2):
                load_at(48 + n, w_out_piece(n), n % 3)
            b, use = Turn(45, 3, 0).tile(3)
            sp.wait_ge(acc_full[b], use + 1)
            sp.dma_start(x1[:], x_tok).then_inc(x1_loaded, 16)
            sp.dma_start(r_bias[:], router_bias[0:1, :].broadcast_to([P, E])).then_inc(rb_loaded, 16)

            for n in range(2, 4):
                load_at(48 + n, w_out_piece(n), n % 3)
                if n == 2:
                    sp.wait_ge(mixl_done, KD)
                    sp.dma_start(ln_g[:], ln1_g[0:1, :].broadcast_to([P, D])).then_inc(ln_loaded, 16)
                    sp.dma_start(ln_b[:], ln1_b[0:1, :].broadcast_to([P, D])).then_inc(ln_loaded, 16)
            load_at(52, by_row(w_router[0]), 1)
            load_at(53, by_row(w_su[0]), 2)
            load_at(54, by_row(w_sg[0]), 0)
            load_at(55, by_row(w_sd[0]), 1)
            for tt in range(NT):
                sp.wait_ge(x1_done[tt], 1)
                sp.dma_start(x1_dram[P * tt:P * (tt + 1), :], x1[:, tt, :]).then_inc(x1_stored, 16)
            for n in range(4):
                load_at(56 + n, by_row(w_pg[0])[:, :, COLS * n:COLS * (n + 1)], (56 + n) % 3)

            def load_weight(i, b, s, first=False):
                n = 60 + 3 * (2 * i + b) + s
                sp.wait_ge(lo_done, n - (2 if first and b == 0 else 5))
                if not isinstance(i, int):
                    sp.sem_inc(loads_issued, 1)
                src = (w_eg, w_eu, w_ed)[s][0].rearrange("e (p k) n -> p e (k n)", p=P)[:, bass.ds(2 * i + b, 1), :]
                sp.dma_start(raw[:, 3 * b + s:3 * b + s + 1, :], src).then_inc(raw_full[3 * b + s], 16)

            def load_expert(i, b, first=False):
                for s in range(3):
                    load_weight(i, b, s, first)

            for b in range(2):
                load_expert(0, b, first=True)
            y_rows = y_dram.rearrange("(t p) d -> p t d", p=P)

            def store_y(n):
                cols = slice(COLS * n, COLS * (n + 1))
                sp.wait_ge(ple_done, 4 * (n + 1))
                sp.dma_start(y_rows[:, :, cols], y_acc[:, :, cols]).then_inc(y_stored, 16)

            store_y(0)
            store_y(1)
            load_weight(1, 0, 0)
            store_y(2)
            load_weight(1, 0, 1)
            store_y(3)
            load_weight(1, 0, 2)
            load_expert(1, 1)
            with sp.Fori(2, E // 2) as i:
                for b in range(2):
                    load_expert(i, b)

            sp.wait_ge(y_ready, E)
            sp.dma_start(tail_s[0][:], ln2_g[0:1, :].broadcast_to([P, D])).then_inc(ln2_loaded, 16)
            sp.dma_start(tail_s[1][:], ln2_b[0:1, :].broadcast_to([P, D])).then_inc(ln2_loaded, 16)
            sp.wait_ge(y_free, 2 + E)
            def over_sp(e, r, n):
                for s, w in enumerate((w_eg, w_eu, w_ed)):
                    sp.wait_ge(over_done, n)
                    sp.sem_inc(loads_issued, 1)
                    src = w[0].rearrange("e (p k) n -> p e (k n)", p=P)[:, bass.ds(e, 1), :]
                    sp.dma_start(raw[:, s:s + 1, :], src).then_inc(over_loaded, 16)

            further_rounds(sp, over_sp)
            sp.wait_ge(rounds_over, 1)
            for tt in range(NT):
                sp.dma_start(y_acc[:, tt, :], y_rows[:, tt, :]).then_inc(y_loaded[tt], 16)
            out_tok = out[0].rearrange("(t p) d -> p t d", p=P)
            for tt in range(NT):
                sp.wait_ge(out_done[tt], 1)
                sp.dma_start(out_tok[:, tt, :], y_acc[:, tt, :]).then_inc(out_stored, 16)
            sp.wait_ge(out_stored, 16 * NT)

        @block.gpsimd
        def _(pool):
            ch = Chain(pool, pool_chain)
            nc.gpsimd.memset(one_col[:], 1.0).then_inc(consts_made, 1)
            ch.link(nc.gpsimd.memset(ones_f[:], 1.0))
            ch.link(nc.gpsimd.memset(ident[:], 0.0))
            nc.gpsimd.affine_select(out=ident[:], in_=ident[:], compare_op=ALU.not_equal, fill=1.0, base=0,
                                    pattern=[[-1, P]], channel_multiplier=1).then_inc(consts_made, 1)
            nc.gpsimd.affine_select(out=causal[:], in_=ones_f[:], compare_op=ALU.is_ge, fill=0.0, base=0,
                                    pattern=[[1, P]], channel_multiplier=-1).then_inc(consts_made, 1)
            pool.wait_ge(consts_made, 5)
            with pool.Fori(0, 4) as i:
                for hl in range(2):
                    for a in range(NT):
                        if a == 0:
                            pool.wait_ge(exp_done, 2 * i + hl + 1)
                        blk = decay[:, hl, SEG[a]:SEG[a] + P]
                        nc.gpsimd.tensor_tensor(blk, blk, causal[:], ALU.mult).then_inc(mask_done, 1)
            pool.wait_ge(mixl_done, KD)
            nc.gpsimd.iota(iota_i[:], pattern=[[1, P]], base=0, channel_multiplier=0).then_inc(iota_done, 1)
            nc.gpsimd.iota(iota_s[:], pattern=[[1, 8], [-1, 8]], base=0, channel_multiplier=0).then_inc(iota_done, 1)
            nc.gpsimd.iota(iota_t[:], pattern=[[P, NT]], base=-OOB, channel_multiplier=1).then_inc(iota_done, 1)
            pool.wait_ge(x1_stored, 16 * NT)
            pool.wait_ge(x1T_ready, KD)
            pool.wait_ge(y_init, NT)
            for b in range(2):
                nc.gpsimd.memset(xg[b][:], 0.0).then_inc(xg_clear, 1)
            gathered, scattered = (gathered0, gathered1), (scattered0, scattered1)

            def gather(b):
                nc.gpsimd.indirect_dma_start(out=xg[b][:], out_offset=None, in_=x1_dram,
                                             in_offset=bass.IndirectOffsetOnAxis(ap=tok_idx[b][:, 0:1], axis=0),
                                             bounds_check=SEQ - 1, oob_is_err=False).then_inc(gathered[b], 16)

            def scatter(b):
                nc.gpsimd.indirect_dma_start(out=y_dram, in_=y_out[b][:], in_offset=None,
                                             out_offset=bass.IndirectOffsetOnAxis(ap=dst_idx[b][:, 0:1], axis=0),
                                             bounds_check=SEQ - 1, oob_is_err=False, compute_op=ALU.add).then_inc(scattered[b], 16)

            pool.wait_ge(xg_clear, 2)
            pool.sem_inc(y_free, 1)
            for b in range(2):
                pool.wait_ge(idx_done, b + 1)
                gather(b)

            def expert_pool(x, back, ahead, tables):
                if tables:
                    pool.wait_ge(idx_done, x.e + 3)
                    pool.wait_ge(xgT_ready, x.e + 1)
                    pool.sem_inc(pool_tick, 1)
                    gather(x.par)
                if back:
                    if not (isinstance(x.i, int) and x.i == 0):
                        pool.wait_ge(scattered[x.par], 16 * x.i)
                    else:
                        pool.wait_ge(y_stored, 64)
                    pool.sem_inc(y_free, 1)
                    pool.wait_ge(dst_done, x.e)
                    pool.wait_ge(y_done, 2 * x.e + 1)
                    pool.sem_inc(pool_tick, 1)
                    scatter(1 - x.par)

            run_experts(pool, expert_pool, E)
            pool.wait_ge(scattered1, 16 * (E // 2))
            pool.sem_inc(y_free, 1)

            def over_pool(e, r, n):
                pool.wait_ge(over_lists, n)
                pool.wait_ge(over_done, n)
                pool.sem_inc(pool_tick, 1)
                nc.gpsimd.indirect_dma_start(out=xg[0][:], out_offset=None, in_=x1_dram,
                                             in_offset=bass.IndirectOffsetOnAxis(ap=tok_idx[0][:, 0:1], axis=0),
                                             bounds_check=SEQ - 1, oob_is_err=False).then_inc(over_gathered, 16)
                pool.wait_ge(over_copied, 2 * n)
                pool.sem_inc(pool_tick, 1)
                nc.gpsimd.indirect_dma_start(out=y_dram, in_=y_out[0][:], in_offset=None,
                                             out_offset=bass.IndirectOffsetOnAxis(ap=dst_idx[0][:, 0:1], axis=0),
                                             bounds_check=SEQ - 1, oob_is_err=False, compute_op=ALU.add).then_inc(over_scattered, 16)
                pool.wait_ge(over_scattered, 16 * n)
                pool.sem_inc(over_done, 1)

            pool.sem_inc(over_done, 1)
            further_rounds(pool, over_pool)
            pool.sem_inc(rounds_over, 1)
        @block.scalar
        def _(act):
            def hi(turn, s):
                slot = s % 3
                n = turn.piece(s)
                act.wait_ge(raw_full[slot], 16 * (turn.third(s) + 1))
                if not (isinstance(n, int) and n < 3):
                    b, use = turn.tile(2 * (s - 3) + 1)
                    act.wait_ge(acc_full[b], use + 1)
                nc.scalar.activation(split_hi[:, slot, :], raw[:, slot, :], ACT.Copy).then_inc(hi_done, 1)

            act.sem_inc(tr_done, 1)
            act.sem_inc(y_done, 1)
            for kk in range(KD):
                act.wait_ge(xT_ready, kk + 1)
                nc.scalar.activation(xT_hi[:, kk, :], bank[kk][:], ACT.Copy).then_inc(xT_hi_done, 1)
                if kk == 0:
                    act.wait_ge(small_loaded, 16 * 5)
                    nc.scalar.activation(wg_hi[:], wg_raw[:], ACT.Copy).then_inc(wg_split, 1)
            for s in range(3):
                hi(Turn(0, 3, 0), s)
            for kk in range(KF):
                act.wait_ge(xT_ready, KD + kk + 1)
                nc.scalar.activation(pT_hi[:, kk, :], bank[kk][:], ACT.Copy).then_inc(xT_hi_done, 1)
            act.wait_ge(gate_step, 1)
            nc.scalar.activation(gt[2][:], gt[2][:], ACT.Exp, scale=-1.0).then_inc(gate_fn, 1)
            act.wait_ge(gate_fn, 1)
            act.wait_ge(consts_made, 1)
            nc.scalar.activation(gt[2][:], gt[2][:], ACT.Ln, bias=one_col[0:HEADS, :]).then_inc(gate_fn, 1)
            act.wait_ge(gate_step, 2)
            nc.scalar.activation(gt[4][:], gt[4][:], ACT.Exp, scale=-1.0).then_inc(gate_fn, 1)

            def mixer_turn(i):
                t = Turn(0, 6, i)

                def evac(tile, out_, **kw):
                    b, use = t.tile(tile)
                    act.wait_ge(acc_full[b], use + 1)
                    return nc.scalar.activation(out_, bank[b][:], ACT.Copy, **kw)

                for m in range(2):
                    evac(m, qT[:, m, :], scale=QK_SCALE).then_inc(acc_free[m % 3], 1)
                hi(t, 3)

                def squares(hl):
                    act.wait_ge(num_ready, 2 * i + hl + 1)
                    for j in range(NT):
                        b, c0 = NUM_PLACE[j]
                        nc.scalar.activation(head_out[:, j, :], b[:, c0:c0 + DH], ACT.Square,
                                             accum_out=hs[:, 0, j:j + 1]).then_inc(sq_done, 1)

                def weights(hl):
                    act.wait_ge(arg_done, 8 * i + 4 * hl + 4)
                    nc.scalar.activation(decay[:, hl, :], decay[:, hl, :], ACT.Exp, scale=-1.0).then_inc(exp_done, 1)

                def rsqrt_seed(hl):
                    act.wait_ge(ln_in, 2 * i + hl + 1)
                    nc.scalar.activation(hs[:, 5, :], hs[:, 4, :], ACT.Ln).then_inc(ln_out, 1)
                    act.wait_ge(ln_out, 4 * i + 2 * hl + 1)
                    nc.scalar.activation(hs[:, 6, :], hs[:, 5, :], ACT.Exp, scale=-0.5).then_inc(ln_out, 1)

                def head_back(hl):
                    act.wait_ge(tr_ready, 2 * i + hl + 1)
                    nc.scalar.activation(hT[:, bass.ds(2 * i + hl, 1), :],
                                         MB[:].rearrange("p (a n) -> p a n", a=1), ACT.Copy).then_inc(tr_done, 1)

                def conv_gated(m):
                    b, use = t.tile(10 + m)
                    act.wait_ge(acc_free[b], use + 2)

                evac(2, kT[:, 0, :]).then_inc(acc_free[2], 1)
                weights(0)
                evac(3, kT[:, 1, :]).then_inc(acc_free[0], 1)
                hi(t, 4)
                hi(t, 5)
                act.wait_ge(ya_lo_done, 2 * i + 1)
                evac(6, conv_c[:, 0, :]).then_inc(acc_free[0], 1)
                squares(0)
                weights(1)
                rsqrt_seed(0)
                evac(7, conv_c[:, 1, :]).then_inc(acc_free[1], 1)
                hi(t, 6)
                head_back(0)
                hi(t, 7)
                squares(1)
                rsqrt_seed(1)
                conv_gated(0)
                nc.scalar.activation(yaT_hi[:, bass.ds(2 * i, 1), :], conv_c[:, 0:1, :], ACT.Copy).then_inc(ya_hi_done, 1)
                conv_gated(1)
                nc.scalar.activation(yaT_hi[:, bass.ds(2 * i + 1, 1), :], conv_c[:, 1:2, :], ACT.Copy).then_inc(ya_hi_done, 1)
                head_back(1)
                hi(t, 8)

            mixer_turn(0)
            with act.Fori(1, 4) as i:
                mixer_turn(i)

            with act.Fori(0, 4) as i:
                t = Turn(24, 3, i)
                for m in range(2):
                    b, use = t.tile(m)
                    act.wait_ge(acc_full[b], use + 1)
                    act.wait_ge(mixa_done, 2 * i + m + 1)
                    nc.scalar.activation(branch[:, m, :], bank[b][:], ACT.Copy).then_inc(acc_free[b], 1)
                hi(t, 3)
                for m in range(2):
                    b, use = t.tile(2 + m)
                    act.wait_ge(acc_full[b], use + 1)
                    nc.scalar.activation(merge_g[:, m, :], bank[b][:], ACT.Sigmoid).then_inc(acc_free[b], 1)
                hi(t, 4)
                for m in range(2):
                    b, use = t.tile(4 + m)
                    act.wait_ge(acc_full[b], use + 1)
                    act.wait_ge(ybl_done, 2 * i + m + 1)
                    nc.scalar.activation(yb_tmp[:, m, :], bank[b][:], ACT.Sigmoid).then_inc(acc_free[b], 1)
                hi(t, 5)
                for m in range(2):
                    act.wait_ge(yb_done, 2 * i + m + 1)
                    nc.scalar.activation(ybT_hi[:, bass.ds(2 * i + m, 1), :], yb_tmp[:, m:m + 1, :], ACT.Copy).then_inc(ybh_done, 1)

            act.wait_ge(mixa_done, 2 + KD)
            with act.Fori(0, 4) as i:
                t = Turn(36, 3, i)
                for m in range(2):
                    b, use = t.tile(m)
                    act.wait_ge(acc_full[b], use + 1)
                    nc.scalar.activation(ple_proj[:, 2 * m:2 * m + 2, bass.ds(COLS * i, COLS)],
                                         bank[b][:].rearrange("p (t n) -> p t n", t=2), ACT.Copy).then_inc(acc_free[b], 1)
                hi(t, 3)
                for m in range(2):
                    b, use = t.tile(2 + m)
                    act.wait_ge(acc_full[b], use + 1)
                    nc.scalar.activation(merge_g[:, m, :], bank[b][:], ACT.Sigmoid).then_inc(acc_free[b], 1)
                hi(t, 4)
                for m in range(2):
                    act.wait_ge(mix_done, 2 * i + m + 1)
                    nc.scalar.activation(mix_hi[:, bass.ds(2 * i + m, 1), :], branch[:, m:m + 1, :], ACT.Copy).then_inc(mixh_done, 1)
                hi(t, 5)

            def hi_at(n, free=None, width=2048):
                act.wait_ge(raw_full[n % 3], 16 * (n // 3 + 1))
                if free:
                    act.wait_ge(*free)
                nc.scalar.activation(split_hi[:, n % 3, 0:width], raw[:, n % 3, 0:width], ACT.Copy).then_inc(hi_done, 1)

            def std_act(k):
                act.wait_ge(seed_in, k)
                nc.scalar.activation(ln_s[:, 1, :], ln_s[:, 0, :], ACT.Sqrt).then_inc(seed_out, 1)

            def normalise_last(k, rows, done):
                act.wait_ge(moments_done, k)
                nc.scalar.activation(rows[:, NT - 1, :], rows[:, NT - 1, :], ACT.Identity, bias=ln_s[:, 5, NT - 1:NT],
                                     scale=ln_s[:, 4, NT - 1:NT]).then_inc(done, 1)

            out_turn = Turn(48, 12, 0)
            def w_out_used(s):
                b, use = out_turn.tile(2 * s + 1)
                return acc_full[b], use + 1

            hi_at(51, w_out_used(0))
            act.wait_ge(raw_full[1], 16 * (52 // 3 + 1))
            nc.scalar.activation(router_hi[:], raw[:, 1, 0:KD * E], ACT.Copy).then_inc(hi_done, 1)
            hi_at(53, w_out_used(2))
            hi_at(54, w_out_used(3))
            std_act(1)
            normalise_last(1, x1, x1_scaled)
            for tt in range(NT):
                act.wait_ge(x1_done[tt], 1)
                nc.scalar.activation(y_acc[:, tt, :], x1[:, tt, :], ACT.Copy, scale=ALPHA).then_inc(y_init, 1)
            for kk in range(KD):
                act.wait_ge(x1T_ready, kk + 1)
                nc.scalar.activation(x1T_hi[:, kk, :], bank[kk][:], ACT.Copy).then_inc(x1T_hi_done, 1)
            hi_at(55)
            act.wait_ge(router_ready, 1)
            nc.scalar.activation(logits_t[:], bank[0][0:E, :], ACT.Copy).then_inc(scores_done, 1)
            act.wait_ge(router_ready, 2)
            nc.scalar.activation(scores_s[:].rearrange("p t e -> p (t e)"), bank[1][:, 0:NT * E], ACT.Sigmoid).then_inc(scores_done, 1)
            for tt in range(NT):
                act.wait_ge(sh_ready, tt + 1)
                if tt:
                    act.wait_ge(sh_done, tt)
                nc.scalar.activation(sh_s[:], bank[3 + tt][:, 0:F], ACT.Silu).then_inc(sh_silu, 1)
            for kk in range(KF):
                act.wait_ge(shT_ready, kk + 1)
                nc.scalar.activation(shT_hi[:, kk, :], bank[7 if kk == 0 else 2][:], ACT.Copy).then_inc(shT_hi_done, 1)
            hi_at(56)
            hi_at(57)
            hi_at(58, (shd_ready, 8))
            def gathered_hi(x):
                act.wait_ge(xgT_ready, x.e + 1)
                for half in range(2):
                    nc.scalar.activation(xgT_hi[x.par][:, 4 * half:4 * half + 4, :].rearrange("p k n -> p (k n)"), bank[2 + half][:],
                                         ACT.Copy).then_inc(xgTh_done, 1)

            for n in range(4):
                for m in range(2):
                    k = 2 * n + m
                    if k == 7:
                        gathered_hi(Expert(0, 0))
                    act.wait_ge(ple_ready[k % 3], k // 3 + 1)
                    if k >= 2:
                        act.wait_ge(ple_done, 2 * (k - 1))
                    nc.scalar.activation(ple_s[:, m, :], bank[k % 3][:], ACT.Sigmoid).then_inc(ple_sig, 1)
                k = 2 * n + 1
                hi_at(59 + n, (ple_ready[k % 3], k // 3 + 1))

            sets_hi = (split_hi, split_hi_b)

            def expert_hi(x, s):
                slot = 3 * x.par + s
                act.wait_ge(raw_full[slot], 16 * (x.i + 1) if x.par else 16 * (x.i + 21))
                nc.scalar.activation(sets_hi[x.par][:, s, :], raw[:, slot, :], ACT.Copy).then_inc(hi_done, 1)

            act.wait_ge(ple_done, 16)

            def expert_act(x, back, ahead, tables):
                if ahead:
                    expert_hi(x.next(), 0)
                if back:
                    act.wait_ge(exT_ready, x.e)
                    nc.scalar.activation(exT_hi[:].rearrange("p k n -> p (k n)"), bank[4][:, 0:KF * P], ACT.Copy).then_inc(exTh_done, 1)
                if ahead:
                    gathered_hi(x.next())
                    expert_hi(x.next(), 1)
                if ahead or x.par:
                    act.wait_ge(gu_ready, x.e + 1)
                    nc.scalar.activation(ex_h[:], bank[x.par][:, 0:F], ACT.Silu).then_inc(silu_done, 1)
                if back:
                    act.wait_ge(y_ready, x.e)
                    act.wait_ge(y_free, x.e)
                    for half in range(2):
                        nc.scalar.activation(y_out[1 - x.par][:, 512 * half:512 * (half + 1)], bank[6 + half][:], ACT.Copy).then_inc(y_done, 1)
                if ahead:
                    expert_hi(x.next(), 2)

            run_experts(act, expert_act, E)

            def over_act(e, r, n):
                for s in range(3):
                    act.wait_ge(over_loaded, 48 * n)
                    nc.scalar.activation(split_hi[:, s, :], raw[:, s, :], ACT.Copy).then_inc(over_hi, 1)
                act.wait_ge(over_turned, n)
                for half in range(2):
                    nc.scalar.activation(xgT_hi[0][:, 4 * half:4 * half + 4, :].rearrange("p k n -> p (k n)"), bank[2 + half][:],
                                         ACT.Copy).then_inc(over_xh, 1)
                act.wait_ge(over_gu, n)
                nc.scalar.activation(ex_h[:], bank[0][:, 0:F], ACT.Silu).then_inc(over_silu, 1)
                act.wait_ge(over_exT, n)
                nc.scalar.activation(exT_hi[:].rearrange("p k n -> p (k n)"), bank[4][:, 0:KF * P], ACT.Copy).then_inc(over_exh, 1)
                act.wait_ge(over_y, n)
                for half in range(2):
                    nc.scalar.activation(y_out[0][:, 512 * half:512 * (half + 1)], bank[6 + half][:], ACT.Copy).then_inc(over_copied, 1)

            further_rounds(act, over_act)
            std_act(2)
            normalise_last(2, y_acc, y_scaled)

        @block.vector
        def _(dve):
            ch = Chain(dve, dve_chain)

            def lo(turn, s):
                slot = s % 3
                dve.wait_ge(hi_done, turn.piece(s) + 1)
                nc.vector.tensor_tensor(split_lo[:, slot, :], raw[:, slot, :], split_hi[:, slot, :].bitcast(F32),
                                        ALU.subtract).then_inc(lo_done, 1)

            dve.sem_inc(ya_lo_done, 1)
            dve.sem_inc(mixa_done, 2)
            dve.sem_inc(ybl_done, 2)
            dve.memset(conv_u[:, :, 0:2], 0.0).then_inc(consts_made, 1)
            dve.memset(v_ext[:, :, :, DH:DH + 2], 1.0).then_inc(consts_made, 1)
            for kk in range(KD):
                dve.wait_ge(xT_hi_done, kk + 1)
                nc.vector.tensor_tensor(xT_lo[:, kk, :], bank[kk][:], xT_hi[:, kk, :].bitcast(F32), ALU.subtract).then_inc(xT_lo_done, 1)
            dve.wait_ge(wg_split, 1)
            nc.vector.tensor_tensor(wg_lo[:], wg_raw[:], wg_hi[:].bitcast(F32), ALU.subtract).then_inc(wg_split, 1)
            for s in range(3):
                lo(Turn(0, 3, 0), s)
            for kk in range(KF):
                dve.wait_ge(xT_hi_done, KD + kk + 1)
                nc.vector.tensor_tensor(pT_lo[:, kk, :], bank[kk][:], pT_hi[:, kk, :].bitcast(F32), ALU.subtract).then_inc(xT_lo_done, 1)
            dve.wait_ge(gates_ready, 1)
            nc.vector.tensor_copy(params[:], bank[5][:, 0:32]).then_inc(gates_used, 1)
            i_pre, nabs, f_pre, logf, run_sum, tmp = gt[0], gt[2], gt[1], gt[3], gt[4], gt[5]
            ch.link(nc.vector.tensor_scalar(i_pre[:], bank[3][0:HEADS, :], bias_if[:, 0:1], None, ALU.add))
            ch.link(nc.vector.tensor_scalar(f_pre[:], bank[4][0:HEADS, :], bias_if[:, 1:2], None, ALU.add))
            nc.vector.scalar_tensor_tensor(nabs[:], f_pre[:], -1.0, f_pre[:], ALU.mult, ALU.max).then_inc(gate_step, 1)
            dve.wait_ge(gate_fn, 2)
            ch.link(nc.vector.scalar_tensor_tensor(logf[:], f_pre[:], 0.0, nabs[:], ALU.min, ALU.subtract))
            ch.link(nc.vector.tensor_tensor_scan(tmp[:], logf[:], logf[:], 0.0, ALU.add, ALU.bypass))
            ch.link(nc.vector.tensor_tensor(i_pre[:], i_pre[:], tmp[:], ALU.subtract))
            ch.link(nc.vector.tensor_tensor_scan(run_max[:], i_pre[:], i_pre[:], 0.0, ALU.max, ALU.bypass))
            nc.vector.tensor_tensor(run_sum[:], tmp[:], run_max[:], ALU.add).then_inc(gate_step, 1)
            dve.wait_ge(gates_ready, 2)
            nc.vector.tensor_copy(g_tok[:].rearrange("p t h -> p (t h)"), bank[6][:, 0:NT * HEADS]).then_inc(gates_used, 1)
            nc.vector.tensor_copy(guard[:].rearrange("p t h -> p (t h)"), bank[6][:, 64:64 + NT * HEADS]).then_inc(gates_used, 1)
            dve.wait_ge(gates_used, 3)

            def mixer_turn(i):
                t = Turn(0, 6, i)
                h_of = lambda hl: bass.ds(2 * i + hl, 1)

                def acc(tile):
                    b, use = t.tile(tile)
                    dve.wait_ge(acc_full[b], use + 1)
                    return bank[b][:], acc_free[b]

                def select_max(hl):
                    nc.vector.tensor_scalar(max_sel[:, hl, :], run_max[:], ident[0:HEADS, h_of(hl)], None, ALU.mult).then_inc(sel_done, 1)

                def exponents(hl):
                    dve.wait_ge(mb_ready, 2 * i + hl + 1)
                    for a in range(NT):
                        nc.vector.tensor_scalar(decay[:, hl, SEG[a]:SEG[a] + SEQ - P * a], MB[:, P * a:SEQ],
                                                g_tok[:, a, h_of(hl)], 0.0, ALU.subtract, ALU.max).then_inc(arg_done, 1)

                def scores(hl):
                    dve.wait_ge(s_ready, 2 * i + hl + 1)
                    dve.wait_ge(mask_done, 8 * i + 4 * hl + 4)
                    for a in range(NT):
                        b, c0 = S_PLACE[a]
                        seg = decay[:, hl, SEG[a]:SEG[a] + SEQ - P * a]
                        nc.vector.tensor_tensor(seg, b[:, c0:c0 + SEQ - P * a], seg, ALU.mult).then_inc(pt_done, 1)

                def normalise(hl, meanwhile=None):
                    dve.wait_ge(sq_done, 8 * i + 4 * hl + 4)
                    den3 = NUM[:, 0:390].rearrange("p (j n) -> p j n", j=3)[:, :, DH]
                    for cols, den in ((slice(0, 3), den3), (slice(3, 4), S2[:, 256 + DH:257 + DH])):
                        ch.link(nc.vector.scalar_tensor_tensor(hs[:, 1, cols], den, -1.0, guard[:, cols, 2 * i + hl], ALU.mult, ALU.max))
                        ch.link(nc.vector.tensor_tensor(hs[:, 1, cols], den, hs[:, 1, cols], ALU.max))
                    ch.link(nc.vector.reciprocal(hs[:, 2, :], hs[:, 1, :]))
                    ch.link(nc.vector.tensor_tensor(hs[:, 3, :], hs[:, 2, :], hs[:, 2, :], ALU.mult))
                    ch.link(nc.vector.scalar_tensor_tensor(hs[:, 3, :], hs[:, 0, :], 1.0 / DH, hs[:, 3, :], ALU.mult, ALU.mult))
                    nc.vector.tensor_scalar(hs[:, 4, :], hs[:, 3, :], RMS_EPS, None, ALU.add).then_inc(ln_in, 1)
                    if meanwhile:
                        meanwhile()
                    dve.wait_ge(ln_out, 4 * i + 2 * hl + 2)
                    ch.link(nc.vector.tensor_tensor(hs[:, 7, :], hs[:, 6, :], hs[:, 6, :], ALU.mult))
                    ch.link(nc.vector.tensor_tensor(hs[:, 7, :], hs[:, 7, :], hs[:, 4, :], ALU.mult))
                    ch.link(nc.vector.tensor_scalar(hs[:, 7, :], hs[:, 7, :], -0.5, 1.5, ALU.mult, ALU.add))
                    ch.link(nc.vector.tensor_tensor(hs[:, 7, :], hs[:, 7, :], hs[:, 6, :], ALU.mult))
                    ch.link(nc.vector.tensor_tensor(hs[:, 8, :], hs[:, 7, :], hs[:, 2, :], ALU.mult))
                    for j in range(NT):
                        b, c0 = NUM_PLACE[j]
                        nc.vector.tensor_scalar(head_out[:, j, :], b[:, c0:c0 + DH], hs[:, 8, j:j + 1], None, ALU.mult).then_inc(head_done, 1)

                def v_tokens(m):
                    src, free = acc(4 + m)
                    nc.vector.tensor_copy(v_ext[:, 2 * m:2 * m + 2, :, 0:DH], src.rearrange("p (t h d) -> p t h d", t=2, h=2)).then_inc(free, 1)

                select_max(0)
                select_max(1)
                lo(t, 3)
                exponents(0)
                lo(t, 4)
                v_tokens(0)
                scores(0)
                v_tokens(1)
                lo(t, 5)

                def gate_in(m):
                    src, free = acc(8 + m)
                    b, use = t.tile(6 + m)
                    dve.wait_ge(acc_free[b], use + 2)
                    nc.vector.tensor_tensor(conv_u[:, m, 2:SEQ + 2], src, conv_c[:, m, :], ALU.mult).then_inc(free, 1)

                def conv(m):
                    w = lambda j: params[:, bass.ds(8 * j + m + 2 * i, 1)]
                    b, use = t.tile(8 + m)
                    dve.wait_ge(acc_free[b], use + 2)
                    ch.link(nc.vector.tensor_scalar(conv_c[:, m, :], conv_u[:, m, 0:SEQ], w(0), None, ALU.mult))
                    for j in (1, 2):
                        ch.link(nc.vector.scalar_tensor_tensor(conv_c[:, m, :], conv_u[:, m, j:j + SEQ], w(j), conv_c[:, m, :], ALU.mult, ALU.add))

                def gate_out(m):
                    src, free = acc(10 + m)
                    nc.vector.tensor_tensor(conv_c[:, m, :], src, conv_c[:, m, :], ALU.mult).then_inc(free, 1)

                def ya_lo(m):
                    dve.wait_ge(ya_hi_done, 2 * i + m + 1)
                    nc.vector.tensor_tensor(yaT_lo[:, bass.ds(2 * i + m, 1), :], conv_c[:, m:m + 1, :],
                                            yaT_hi[:, bass.ds(2 * i + m, 1), :].bitcast(F32), ALU.subtract).then_inc(ya_lo_done, 1)

                exponents(1)
                normalise(0)
                lo(t, 6)
                gate_in(0)
                scores(1)
                conv(0)
                gate_in(1)
                lo(t, 7)
                normalise(1, meanwhile=lambda: conv(1))
                gate_out(0)
                ya_lo(0)
                gate_out(1)
                ya_lo(1)
                lo(t, 8)

            mixer_turn(0)
            with dve.Fori(1, 4) as i:
                ch.enter_loop(i - 1, 30)
                mixer_turn(i)
                ch.leave_loop(3)

            def ready(turn, tile):
                b, use = turn.tile(tile)
                dve.wait_ge(acc_free[b], use + 2)

            dve.wait_ge(tr_done, 1 + HEADS)
            with dve.Fori(0, 4) as i:
                t = Turn(24, 3, i)
                c = lambda m: bass.ds(2 * i + m, 1)
                lo(t, 3)
                for m in range(2):
                    ready(t, 2 + m)
                    nc.vector.tensor_tensor(mixed_a[:, c(m), :], branch[:, m:m + 1, :], merge_g[:, m:m + 1, :], ALU.mult).then_inc(mixa_done, 1)
                lo(t, 4)
                for m in range(2):
                    ready(t, 4 + m)
                    nc.vector.scalar_tensor_tensor(yb_tmp[:, m:m + 1, :], hT[:, c(m), :], params[:, bass.ds(2 * i + m + 24, 1)],
                                                   yb_tmp[:, m:m + 1, :], ALU.mult, ALU.mult).then_inc(yb_done, 1)
                lo(t, 5)
                for m in range(2):
                    dve.wait_ge(ybh_done, 2 * i + m + 1)
                    nc.vector.tensor_tensor(ybT_lo[:, c(m), :], yb_tmp[:, m:m + 1, :], ybT_hi[:, c(m), :].bitcast(F32), ALU.subtract).then_inc(ybl_done, 1)

            with dve.Fori(0, 4) as i:
                t = Turn(36, 3, i)
                c = lambda m: bass.ds(2 * i + m, 1)
                lo(t, 3)
                lo(t, 4)
                for m in range(2):
                    b, use = t.tile(4 + m)
                    ready(t, 2 + m)
                    dve.wait_ge(acc_full[b], use + 1)
                    nc.vector.tensor_tensor(branch[:, m, :], bank[b][:], merge_g[:, m, :], ALU.mult).then_inc(acc_free[b], 1)
                    dve.wait_ge(acc_free[b], use + 2)
                    nc.vector.tensor_tensor(branch[:, m:m + 1, :], branch[:, m:m + 1, :], mixed_a[:, c(m), :], ALU.add).then_inc(mix_done, 1)
                for m in range(2):
                    dve.wait_ge(mixh_done, 2 * i + m + 1)
                    nc.vector.tensor_tensor(mix_lo[:, c(m), :], branch[:, m:m + 1, :], mix_hi[:, c(m), :].bitcast(F32), ALU.subtract).then_inc(mixl_done, 1)
                lo(t, 5)

            def lo_at(n, width=2048):
                dve.wait_ge(hi_done, n + 1)
                nc.vector.tensor_tensor(split_lo[:, n % 3, 0:width], raw[:, n % 3, 0:width],
                                        split_hi[:, n % 3, 0:width].bitcast(F32), ALU.subtract).then_inc(lo_done, 1)

            def moments(src, tt):
                for half in range(2):
                    ch.link(nc.vector.bn_stats(bn[:, half, :], src[:, tt, 512 * half:512 * (half + 1)]))
                ch.link(nc.vector.bn_aggr(bn_mv[:, tt, :], bn[:]))

            def rstd(k, meanwhile=None):
                nc.vector.tensor_scalar(ln_s[:, 0, :], bn_mv[:, :, 1], LN_EPS, None, ALU.add).then_inc(seed_in, 1)
                if meanwhile:
                    meanwhile()
                dve.wait_ge(seed_out, k)
                ch.link(nc.vector.reciprocal(ln_s[:, 2, :], ln_s[:, 1, :]))
                y0 = ln_s[:, 2, :]
                ch.link(nc.vector.tensor_tensor(ln_s[:, 3, :], y0, y0, ALU.mult))
                ch.link(nc.vector.tensor_tensor(ln_s[:, 3, :], ln_s[:, 3, :], ln_s[:, 0, :], ALU.mult))
                ch.link(nc.vector.tensor_scalar(ln_s[:, 3, :], ln_s[:, 3, :], -0.5, 1.5, ALU.mult, ALU.add))
                ch.link(nc.vector.tensor_tensor(ln_s[:, 4, :], ln_s[:, 3, :], y0, ALU.mult))
                nc.vector.scalar_tensor_tensor(ln_s[:, 5, :], bn_mv[:, :, 0], -1.0, ln_s[:, 4, :], ALU.mult, ALU.mult).then_inc(moments_done, 1)

            def centre(rows, g):
                for tt in range(NT - 1):
                    ch.add(nc.vector.scalar_tensor_tensor(rows[:, tt, :], rows[:, tt, :], bn_mv[:, tt, 0:1], g[:], ALU.subtract, ALU.mult))
                ch.settle()

            def scale_bias(k, rows, scaled, g, b, done):
                for tt in range(NT - 1):
                    nc.vector.scalar_tensor_tensor(rows[:, tt, :], rows[:, tt, :], ln_s[:, 4, tt:tt + 1], b[:], ALU.mult, ALU.add).then_inc(done[tt], 1)
                    if tt == 0:
                        dve.wait_ge(scaled, 1)
                        ch.link(nc.vector.tensor_tensor(rows[:, NT - 1, :], rows[:, NT - 1, :], g[:], ALU.mult))
                nc.vector.tensor_tensor(rows[:, NT - 1, :], rows[:, NT - 1, :], b[:], ALU.add).then_inc(done[NT - 1], 1)

            dve.wait_ge(iota_done, 3)
            ch.link(nc.vector.tensor_copy(iota_row[:], iota_i[:]))
            ch.link(nc.vector.tensor_scalar(before[:], iota_s[:], 0, None, ALU.is_gt))
            ch.link(nc.vector.tensor_copy(tok_id[:], iota_t[:]))
            ch.link(nc.vector.tensor_tensor(lower_b[:], causal[:], ident[:], ALU.subtract))
            ch.link(nc.vector.tensor_copy(ones_b[:], ones_f[:]))
            ch.link(nc.vector.memset(slot_of[:, :, E:E + 2], -1.0))
            ch.link(nc.vector.memset(route_cols[:].bitcast(F32), 0.0))
            dve.wait_ge(x1_loaded, 16)
            out_turn = Turn(48, 12, 0)
            for s in range(4):
                for m in range(2):
                    b, use = out_turn.tile(2 * s + m)
                    dve.wait_ge(acc_full[b], use + 1)
                    blk = x1[:, 2 * m:2 * m + 2, COLS * s:COLS * (s + 1)]
                    nc.vector.scalar_tensor_tensor(blk, blk, ALPHA, bank[b][:].rearrange("p (t n) -> p t n", t=2),
                                                   ALU.mult, ALU.add).then_inc(acc_free[b], 1)
                    dve.wait_ge(acc_free[b], use + 2)
                    for tt in (2 * m, 2 * m + 1):
                        ch.add(nc.vector.bn_stats(bn_parts[:, tt, s, :], x1[:, tt, COLS * s:COLS * (s + 1)]))
                if s == 1:
                    dve.wait_ge(hi_done, 53)
                    nc.vector.tensor_tensor(router_lo[:], raw[:, 1, 0:KD * E], router_hi[:].bitcast(F32), ALU.subtract).then_inc(lo_done, 1)
                elif s < 3:
                    lo_at(51 + s)
            ch.settle()
            for tt in range(NT):
                ch.add(nc.vector.bn_aggr(bn_mv[:, tt, :], bn_parts[:, tt, :, :]))
            ch.settle()
            dve.wait_ge(ln_loaded, 32)
            rstd(1, meanwhile=lambda: centre(x1, ln_g))
            scale_bias(1, x1, x1_scaled, ln_g, ln_b, x1_done)
            for kk in range(KD):
                dve.wait_ge(x1T_hi_done, kk + 1)
                nc.vector.tensor_tensor(x1T_lo[:, kk, :], bank[kk][:], x1T_hi[:, kk, :].bitcast(F32), ALU.subtract).then_inc(x1T_lo_done, 1)
            lo_at(54)
            lo_at(55)
            dve.wait_ge(scores_done, 2)
            dve.wait_ge(rb_loaded, 16)
            bc = lambda ap, shape: ap.broadcast_to(shape)
            ch.link(nc.vector.tensor_tensor(sel[:], scores_s[:], r_bias[:].rearrange("p (a e) -> p a e", a=1).broadcast_to([P, NT, E]), ALU.add))
            for tg in range(NT * 8):
                ch.add(nc.vector.max(out=top_g[:, tg, :], in_=sel[:].rearrange("p t (g e) -> p (t g) e", g=8)[:, tg, :]))
            ch.settle()
            ch.link(nc.vector.tensor_tensor(gsc[:].rearrange("p t g -> p (t g)"), top_g[:, :, 0], top_g[:, :, 1], ALU.add))
            other = gsc[:].rearrange("p t (a g) -> p t a g", a=1).broadcast_to([P, NT, 8, 8])
            own = gsc[:].rearrange("p t (g a) -> p t g a", a=1).broadcast_to([P, NT, 8, 8])
            ch.link(nc.vector.tensor_tensor(cmp_gt[:], other, own, ALU.is_gt))
            ch.link(nc.vector.tensor_tensor(cmp_eq[:], other, own, ALU.is_equal))
            ch.link(nc.vector.tensor_tensor(cmp_eq[:], cmp_eq[:], before[:].rearrange("p (a g) h -> p a g h", a=1).broadcast_to([P, NT, 8, 8]), ALU.mult))
            ch.link(nc.vector.tensor_tensor(cmp_gt[:], cmp_gt[:], cmp_eq[:], ALU.add))
            ch.link(nc.vector.tensor_reduce(gcnt[:], cmp_gt[:], AX_X, ALU.add))
            ch.link(nc.vector.tensor_scalar(gmask[:], gcnt[:], float(TOP_GROUPS), None, ALU.is_lt))
            ch.link(nc.vector.tensor_scalar(gcnt[:], gmask[:], 1.0, LOW, ALU.subtract, ALU.mult))
            by_group = lambda ap: ap.rearrange("p t (g e) -> p (t g) e", g=8)
            spread = lambda ap: ap.rearrange("p t (g a) -> p (t g) a", a=1).broadcast_to([P, NT * 8, 8])
            ch.link(nc.vector.tensor_tensor(by_group(cand[:]), by_group(sel[:]), spread(gmask[:]), ALU.mult))
            ch.link(nc.vector.tensor_tensor(by_group(cand[:]), by_group(cand[:]), spread(gcnt[:]), ALU.add))
            for tt in range(NT):
                ch.link(nc.vector.max(out=top8[:, tt, :], in_=cand[:, tt, :]))
                ch.link(nc.vector.match_replace(out=rest[:, tt, :], in_to_replace=top8[:, tt, :], in_values=cand[:, tt, :], imm_value=-2 * LOW))
            ch.link(nc.vector.tensor_scalar(chosen[:], rest[:], -2 * LOW, None, ALU.is_equal))
            nc.vector.tensor_copy(chosen_b[:], chosen[:]).then_inc(chosen_done, 1)
            ch.link(nc.vector.tensor_tensor(wsel[:], scores_s[:], chosen[:], ALU.mult))
            ch.link(nc.vector.tensor_reduce(wsum[:, 0, :], wsel[:], AX_X, ALU.add))
            ch.link(nc.vector.reciprocal(wsum[:, 1, :], wsum[:, 0, :]))
            for tt in range(NT):
                ch.link(nc.vector.tensor_scalar(wsel[:, tt, :], wsel[:, tt, :], wsum[:, 1, tt:tt + 1], ROUTED_SCALE, ALU.mult, ALU.mult))
                ch.link(nc.vector.tensor_scalar(route_cols[:, tt, 0:E, 0], chosen[:, tt, :], 0.0, tok_id[:, tt:tt + 1], ALU.mult, ALU.add))
            ch.link(nc.vector.tensor_copy(route_cols[:, :, 0:E, 2], wsel[:]))
            ch.link(nc.vector.tensor_tensor(route_cols[:, :, 0:E, 3], wsel[:], route_cols[:, :, 0:E, 2].bitcast(F32), ALU.subtract))

            def tables():
                dve.wait_ge(pos_ready, 1)
                pos = bank[1][:, 0:NT * E].rearrange("p (t e) -> p t e", t=NT)
                ch.link(nc.vector.scalar_tensor_tensor(slot_1[:], pos, 1.0, chosen[:], ALU.add, ALU.mult))
                ch.link(nc.vector.tensor_scalar(slot_of[:, :, 0:E], slot_1[:], 1.0, None, ALU.subtract))
                ch.link(nc.vector.tensor_reduce(counts[:, 0:1], bank[1][:, NT * E:NT * E + E], AX_X, ALU.max))
                nc.vector.tensor_copy(counts_i[:], counts[:, 0:1]).then_inc(tables_done, 1)

            for tt in range(NT):
                dve.wait_ge(sh_silu, tt + 1)
                nc.vector.tensor_tensor(sh_h[tt][:], bank[3 + tt][:, F:2 * F], sh_s[:], ALU.mult).then_inc(sh_done, 1)
            tables()
            for kk in range(KF):
                dve.wait_ge(shT_hi_done, kk + 1)
                nc.vector.tensor_tensor(shT_lo[:, kk, :], bank[7 if kk == 0 else 2][:], shT_hi[:, kk, :].bitcast(F32), ALU.subtract).then_inc(shT_lo_done, 1)
            dve.wait_ge(y_init, NT)
            for half in range(2):
                for tt in range(NT):
                    k = NT * half + tt
                    dve.wait_ge(shd_ready, k + 1)
                    blk = y_acc[:, tt, 512 * half:512 * (half + 1)]
                    nc.vector.tensor_tensor(blk, bank[3 + tt][:], blk, ALU.add).then_inc(shd_done, 1)
                    if k in (3, 5):
                        lo_at(56 if k == 3 else 57)
            dve.wait_ge(shd_done, 8)
            lo_at(58)

            def one_hot_of(e):
                where = slot_of[:, :, bass.ds(e, 1)].broadcast_to([P, NT, P])
                rows = iota_row[:].rearrange("p (a n) -> p a n", a=1).broadcast_to([P, NT, P])
                nc.vector.tensor_tensor(one_hot[:], rows, where, ALU.is_equal).then_inc(hot_done, 1)

            def slot_lists(b, e, count):
                dve.wait_ge(idx_ready, count)
                nc.vector.tensor_scalar(dst_all[:, bass.ds(e, 1)], bank[5][:, 0:1], float(OOB), None, ALU.add).then_inc(lists_written, 1)
                nc.vector.tensor_reduce(gate_all[:, bass.ds(e, 1)], bank[5][:, 2:4], AX_X, ALU.add).then_inc(lists_written, 1)
                nc.vector.tensor_scalar(tok_idx[b][:], bank[5][:, 0:1], float(OOB), None, ALU.add).then_inc(idx_done, 1)

            def gathered_lo(x):
                for half in range(2):
                    part = lambda t: t[x.par][:, 4 * half:4 * half + 4, :].rearrange("p k n -> p (k n)")
                    dve.wait_ge(xgTh_done, 2 * x.e + half + 1)
                    nc.vector.tensor_tensor(part(xgT_lo), bank[2 + half][:], part(xgT_hi).bitcast(F32), ALU.subtract).then_inc(xgTl_done, 1)

            for n in range(4):
                for m in range(2):
                    k = 2 * n + m
                    if k == 7:
                        gathered_lo(Expert(0, 0))
                        one_hot_of(2)
                    dve.wait_ge(ple_sig, k + 1)
                    s_ = ple_s[:, m, :].rearrange("p (t n) -> p t n", t=2)
                    nc.vector.tensor_tensor(s_, s_, ple_proj[:, 2 * m:2 * m + 2, COLS * n:COLS * (n + 1)], ALU.mult).then_inc(ple_done, 1)
                    dve.wait_ge(ple_done, 2 * k + 1)
                    blk = y_acc[:, 2 * m:2 * m + 2, COLS * n:COLS * (n + 1)]
                    nc.vector.tensor_tensor(blk, blk, s_, ALU.add).then_inc(ple_done, 1)
                lo_at(59 + n)
                if n < 2:
                    one_hot_of(n)
                    slot_lists(n, n, n + 1)

            sets = ((split_hi, split_lo), (split_hi_b, split_lo_b))

            def expert_lo(x, s):
                dve.wait_ge(hi_done, 60 + 3 * x.e + s + 1)
                nc.vector.tensor_tensor(sets[x.par][1][:, s, :], raw[:, 3 * x.par + s, :], sets[x.par][0][:, s, :].bitcast(F32),
                                        ALU.subtract).then_inc(lo_done, 1)

            def expert_dve(x, back, ahead, tables):
                if ahead:
                    expert_lo(x.next(), 0)
                if back:
                    dve.wait_ge(exTh_done, x.e)
                    nc.vector.tensor_tensor(exT_lo[:].rearrange("p k n -> p (k n)"), bank[4][:, 0:KF * P],
                                            exT_hi[:].rearrange("p k n -> p (k n)").bitcast(F32), ALU.subtract).then_inc(exTl_done, 1)
                if tables:
                    slot_lists(x.par, x.e + 2, x.e + 3)
                if ahead:
                    gathered_lo(x.next())
                    expert_lo(x.next(), 1)
                if back:
                    dve.wait_ge(y_free, x.e)
                    nc.vector.tensor_copy(dst_idx[1 - x.par][:], dst_all[:, bass.ds(x.e - 1, 1)]).then_inc(dst_done, 1)
                if ahead or x.par:
                    dve.wait_ge(silu_done, x.e + 1)
                    nc.vector.scalar_tensor_tensor(ex_h[:], bank[x.par][:, F:2 * F], gate_all[:, bass.ds(x.e, 1)], ex_h[:], ALU.mult, ALU.mult).then_inc(h_done, 1)
                if tables:
                    one_hot_of(x.e + 3)
                if ahead:
                    expert_lo(x.next(), 2)

            run_experts(dve, expert_dve, E)

            def over_shift(r):
                dve.wait_ge(over_done, E * (r - 1) + 1)
                nc.vector.tensor_scalar(iota_row[:], iota_row[:], float(P), None, ALU.add).then_inc(over_shifted, 1)
                dve.wait_ge(over_shifted, r)

            def over_dve(e, r, n):
                dve.wait_ge(over_done, n)
                where = slot_of[:, :, bass.ds(e, 1)].broadcast_to([P, NT, P])
                rows = iota_row[:].rearrange("p (a n) -> p a n", a=1).broadcast_to([P, NT, P])
                nc.vector.tensor_tensor(one_hot[:], rows, where, ALU.is_equal).then_inc(over_hot, 1)
                dve.wait_ge(over_lists_ready, n)
                for idx, c in ((tok_idx[0], 0), (dst_idx[0], 0)):
                    nc.vector.tensor_scalar(idx[:], bank[5][:, c:c + 1], float(OOB), None, ALU.add).then_inc(lists_written, 1)
                nc.vector.tensor_reduce(gate_all[:, E:E + 1], bank[5][:, 2:4], AX_X, ALU.add).then_inc(over_lists, 1)
                for s in range(3):
                    dve.wait_ge(over_hi, 3 * n)
                    nc.vector.tensor_tensor(split_lo[:, s, :], raw[:, s, :], split_hi[:, s, :].bitcast(F32), ALU.subtract).then_inc(over_lo, 1)
                dve.wait_ge(over_xh, 2 * n)
                for half in range(2):
                    nc.vector.tensor_tensor(xgT_lo[0][:, 4 * half:4 * half + 4, :].rearrange("p k n -> p (k n)"), bank[2 + half][:],
                                            xgT_hi[0][:, 4 * half:4 * half + 4, :].rearrange("p k n -> p (k n)").bitcast(F32), ALU.subtract).then_inc(over_xl, 1)
                dve.wait_ge(over_silu, n)
                nc.vector.scalar_tensor_tensor(ex_h[:], bank[0][:, F:2 * F], gate_all[:, E:E + 1], ex_h[:], ALU.mult, ALU.mult).then_inc(over_h, 1)
                dve.wait_ge(over_exh, n)
                nc.vector.tensor_tensor(exT_lo[:].rearrange("p k n -> p (k n)"), bank[4][:, 0:KF * P],
                                        exT_hi[:].rearrange("p k n -> p (k n)").bitcast(F32), ALU.subtract).then_inc(over_exl, 1)

            further_rounds(dve, over_dve, before=over_shift)

            dve.wait_ge(ln2_loaded, 32)
            for tt in range(NT):
                dve.wait_ge(y_loaded[tt], 16)
                moments(y_acc, tt)
            rstd(2, meanwhile=lambda: centre(y_acc, tail_s[0]))
            scale_bias(2, y_acc, y_scaled, tail_s[0], tail_s[1], out_done)

        @block.tensor
        def _(pe):
            def product(out_, stat, mov, first, last):
                nc.tensor.matmul(out_, stat[0], mov[0], start=first, stop=False)
                nc.tensor.matmul(out_, stat[0], mov[1], start=False, stop=False)
                return nc.tensor.matmul(out_, stat[1], mov[0], start=False, stop=last)

            def claim(turn, tile):
                b, use = turn.tile(tile)
                pe.wait_ge(acc_free[b], use + 1)
                return b

            def weights_at(s, c0, n):
                return split_hi[:, s % 3, c0:c0 + n], split_lo[:, s % 3, c0:c0 + n]

            def channel_tile(turn, s, m, data, steps=KD):
                if m == 0:
                    pe.wait_ge(lo_done, turn.piece(s) + 1)
                b = claim(turn, 2 * s + m)
                for k in range(steps):
                    mm = product(bank[b][:], weights_at(s, COLS * k + P * m, P), (data[0][:, k, :], data[1][:, k, :]),
                                 k == 0, k == steps - 1)
                mm.then_inc(acc_full[b], 1)

            def token_tile(turn, s, m, data, steps=KD):
                if m == 0:
                    pe.wait_ge(lo_done, turn.piece(s) + 1)
                b = claim(turn, 2 * s + m)
                for t2 in range(2):
                    tok = slice((2 * m + t2) * P, (2 * m + t2 + 1) * P)
                    for k in range(steps):
                        mm = product(bank[b][:, COLS * t2:COLS * (t2 + 1)], (data[0][:, k, tok], data[1][:, k, tok]),
                                     weights_at(s, COLS * k, COLS), k == 0, k == steps - 1)
                mm.then_inc(acc_full[b], 1)

            xT, pT = (xT_hi, xT_lo), (pT_hi, pT_lo)
            pe.wait_ge(consts_made, 5)
            for tt in range(NT):
                pe.wait_ge(x_loaded[tt], 16)
                for kk in range(KD):
                    mm = nc.tensor.transpose(bank[kk][:, P * tt:P * (tt + 1)],
                                             x_in[:, tt, :].rearrange("p (d k) -> p k d", k=KD)[:, kk, :], ident[:])
                    if tt == NT - 1:
                        mm.then_inc(xT_ready, 1)
            pe.wait_ge(wg_split, 2)
            for g in range(2):
                heads = slice(HEADS * g, HEADS * (g + 1))
                for k in range(KD):
                    if g == 0:
                        pe.wait_ge(xT_lo_done, k + 1)
                    mm = product(bank[3 + g][0:HEADS, :], (wg_hi[:, k, heads], wg_lo[:, k, heads]),
                                 (xT_hi[:, k, :], xT_lo[:, k, :]), k == 0, k == KD - 1)
            pe.wait_ge(small_loaded, 16 * 5)
            nc.tensor.transpose(bank[5][:, 0:32], param_rows[:], ident[0:32, 0:32]).then_inc(gates_ready, 1)
            pe.wait_ge(p_loaded, 16)
            for kk in range(KF):
                for tt in range(NT):
                    mm = nc.tensor.transpose(bank[kk][:, P * tt:P * (tt + 1)],
                                             p_in[:, tt, :].rearrange("p (d k) -> p k d", k=KF)[:, kk, :], ident[:])
                mm.then_inc(xT_ready, 1)
            def turn_gates():
                pe.wait_ge(gate_step, 2)
                pe.wait_ge(gate_fn, 3)
                for tt in range(NT):
                    nc.tensor.transpose(MB[:, HEADS * tt:HEADS * (tt + 1)], gt[0][:, P * tt:P * (tt + 1)], ident[0:HEADS, 0:HEADS])
                    mm = nc.tensor.transpose(MB[:, 64 + HEADS * tt:64 + HEADS * (tt + 1)], gt[4][:, P * tt:P * (tt + 1)], ident[0:HEADS, 0:HEADS])
                mm.then_inc(gates_ready, 1)
                pe.wait_ge(gates_used, 3)

            pe.wait_ge(xT_lo_done, KD + KF)
            for b in range(3):
                pe.sem_inc(acc_free[b], 1)

            def mixer_turn(i):
                t = Turn(0, 6, i)

                def spread_max(hl):
                    pe.wait_ge(sel_done, 2 * i + hl + 1)
                    nc.tensor.matmul(MB[:], ones_f[0:HEADS, :], max_sel[:, hl, :], start=True, stop=True).then_inc(mb_ready, 1)

                def score_products(hl):
                    for a in range(NT):
                        b, c0 = S_PLACE[a]
                        mm = nc.tensor.matmul(b[:, c0:c0 + SEQ - P * a], kT[:, hl, P * a:P * (a + 1)],
                                              qT[:, hl, P * a:SEQ], start=True, stop=True)
                    mm.then_inc(s_ready, 1)

                def numerators(hl):
                    pe.wait_ge(pt_done, 8 * i + 4 * hl + 4)
                    for j in range(NT):
                        b, c0 = NUM_PLACE[j]
                        for a in range(j + 1):
                            c = SEG[a] + P * (j - a)
                            mm = nc.tensor.matmul(b[:, c0:c0 + DH + 2], decay[:, hl, c:c + P], v_ext[:, a, hl, :],
                                                  start=(a == 0), stop=(a == j))
                    mm.then_inc(num_ready, 1)

                def turn_head(hl):
                    pe.wait_ge(head_done, 8 * i + 4 * hl + 4)
                    for j in range(NT):
                        mm = nc.tensor.transpose(MB[:, P * j:P * (j + 1)], head_out[:, j, :], ident[:])
                    mm.then_inc(tr_ready, 1)

                def copied(tile):
                    b, use = t.tile(tile)
                    pe.wait_ge(acc_free[b], use + 2)

                channel_tile(t, 0, 0, xT)
                channel_tile(t, 0, 1, xT)
                channel_tile(t, 1, 0, xT)
                if isinstance(i, int):
                    turn_gates()
                pe.wait_ge(tr_done, 2 * i + 1)
                spread_max(0)
                channel_tile(t, 1, 1, xT)
                token_tile(t, 2, 0, xT)
                copied(2)
                score_products(0)
                token_tile(t, 2, 1, xT)
                channel_tile(t, 3, 0, xT)
                copied(5)
                numerators(0)
                pe.wait_ge(arg_done, 8 * i + 4)
                spread_max(1)
                channel_tile(t, 3, 1, xT)
                channel_tile(t, 4, 0, xT)
                pe.wait_ge(head_done, 8 * i + 4)
                score_products(1)
                pe.wait_ge(arg_done, 8 * i + 8)
                turn_head(0)
                channel_tile(t, 4, 1, xT)
                numerators(1)
                channel_tile(t, 5, 0, xT)
                channel_tile(t, 5, 1, xT)
                pe.wait_ge(tr_done, 2 * i + 2)
                turn_head(1)

            mixer_turn(0)
            with pe.Fori(1, 4) as i:
                mixer_turn(i)

            yaT, ybT = (yaT_hi, yaT_lo), (ybT_hi, ybT_lo)
            pe.wait_ge(ya_lo_done, 1 + KD)
            with pe.Fori(0, 4) as i:
                t = Turn(24, 3, i)
                for s, data in enumerate([yaT, xT, xT]):
                    for m in range(2):
                        channel_tile(t, s, m, data)
            with pe.Fori(0, 4) as i:
                t = Turn(36, 3, i)
                for m in range(2):
                    token_tile(t, 0, m, pT, steps=KF)
                for m in range(2):
                    channel_tile(t, 1, m, xT)
                pe.wait_ge(ybl_done, 2 + KD)
                for m in range(2):
                    channel_tile(t, 2, m, ybT)

            mixT, x1T = (mix_hi, mix_lo), (x1T_hi, x1T_lo)
            pe.wait_ge(mixl_done, KD)
            out_turn = Turn(48, 12, 0)
            for s in range(4):
                for m in range(2):
                    token_tile(out_turn, s, m, mixT)
            for b in range(3):
                pe.wait_ge(acc_free[b], 1 + (104 - b + 2) // 3)
            for tt in range(NT):
                pe.wait_ge(x1_done[tt], 1)
                for kk in range(KD):
                    mm = nc.tensor.transpose(bank[kk][:, P * tt:P * (tt + 1)],
                                             x1[:, tt, :].rearrange("p (d k) -> p k d", k=KD)[:, kk, :], ident[:])
                    if tt == NT - 1:
                        mm.then_inc(x1T_ready, 1)
            pe.wait_ge(lo_done, 53)
            for k in range(KD):
                pe.wait_ge(x1T_lo_done, k + 1)
                experts = slice(E * k, E * (k + 1))
                mm = product(bank[0][0:E, :], (router_hi[:, experts], router_lo[:, experts]),
                             (x1T_hi[:, k, :], x1T_lo[:, k, :]), k == 0, k == KD - 1)
            mm.then_inc(router_ready, 1)
            pe.wait_ge(scores_done, 1)
            for tt in range(NT):
                mm = nc.tensor.transpose(bank[1][:, E * tt:E * (tt + 1)], logits_t[:, P * tt:P * (tt + 1)], ident[0:E, 0:E])
            mm.then_inc(router_ready, 1)
            pe.wait_ge(lo_done, 55)
            for tt in range(NT):
                tok = slice(P * tt, P * (tt + 1))
                for k in range(KD):
                    mm = product(bank[3 + tt][:], (x1T_hi[:, k, tok], x1T_lo[:, k, tok]),
                                 (split_hi[:, 0:3:2, F * k:F * (k + 1)], split_lo[:, 0:3:2, F * k:F * (k + 1)]), k == 0, k == KD - 1)
                mm.then_inc(sh_ready, 1)
            pe.wait_ge(chosen_done, 1)
            for tt in range(NT):
                for t2 in range(tt + 1):
                    nc.tensor.matmul(bank[1][:, E * tt:E * (tt + 1)], ones_b[:] if t2 < tt else lower_b[:], chosen_b[:, t2, :],
                                     start=(t2 == 0), stop=(t2 == tt))
            for t2 in range(NT):
                mm = nc.tensor.matmul(bank[1][:, NT * E:(NT + 1) * E], ones_b[:], chosen_b[:, t2, :], start=(t2 == 0), stop=(t2 == NT - 1))
            mm.then_inc(pos_ready, 1)
            for kk in range(KF):
                for tt in range(NT):
                    if kk == 0:
                        pe.wait_ge(sh_done, tt + 1)
                    mm = nc.tensor.transpose(bank[7 if kk == 0 else 2][:, P * tt:P * (tt + 1)],
                                             sh_h[tt][:].rearrange("p (d k) -> p k d", k=KF)[:, kk, :], ident[:])
                mm.then_inc(shT_ready, 1)
            pe.wait_ge(shT_lo_done, KF)
            pe.wait_ge(lo_done, 56)
            for half in range(2):
                for tt in range(NT):
                    if half:
                        pe.wait_ge(shd_done, tt + 1)
                    tok = slice(P * tt, P * (tt + 1))
                    for k in range(KF):
                        mm = product(bank[3 + tt][:], (shT_hi[:, k, tok], shT_lo[:, k, tok]),
                                     weights_at(55, D * k + 512 * half, 512), k == 0, k == KF - 1)
                    mm.then_inc(shd_ready, 1)

            def slot_products(e, count):
                pe.wait_ge(hot_done, count)
                for tt in range(NT):
                    mm = nc.tensor.matmul(bank[5][:, 0:4], one_hot[:, tt, :], route_cols[:, tt, bass.ds(e, 1), :].rearrange("p a c -> p (a c)"),
                                          start=(tt == 0), stop=(tt == NT - 1))
                mm.then_inc(idx_ready, 1)

            def turn_rows(x):
                pe.wait_ge((gathered0, gathered1)[x.par], 16 * (x.i + 1))
                for k in range(KD):
                    mm = nc.tensor.transpose(bank[2 + k // 4][:, P * (k % 4):P * (k % 4 + 1)],
                                             xg[x.par][:].rearrange("p (d k) -> p k d", k=KD)[:, k, :], ident[:])
                mm.then_inc(xgT_ready, 1)

            pe.wait_ge(tables_done, 1)
            for n in range(4):
                pe.wait_ge(lo_done, 57 + n)
                for m in range(2):
                    k = 2 * n + m
                    if k == 7:
                        pe.wait_ge(ple_sig, 6)
                        turn_rows(Expert(0, 0))
                    if k >= 3:
                        pe.wait_ge(ple_sig, k - 2)
                    for t2 in range(2):
                        tok = slice((2 * m + t2) * P, (2 * m + t2 + 1) * P)
                        for kk in range(KD):
                            mm = product(bank[k % 3][:, COLS * t2:COLS * (t2 + 1)], (x1T_hi[:, kk, tok], x1T_lo[:, kk, tok]),
                                         weights_at(56 + n, COLS * kk, COLS), kk == 0, kk == KD - 1)
                    mm.then_inc(ple_ready[k % 3], 1)
                if n in (1, 2):
                    if n == 1:
                        pe.wait_ge(shd_done, 8)
                    slot_products(n - 1, n)

            sets = ((split_hi, split_lo), (split_hi_b, split_lo_b))

            def expert_pe(x, back, ahead, tables):
                def gate_up(first, end):
                    whi, wlo = sets[x.par]
                    for k in range(first, end):
                        mm = product(bank[x.par][:], (xgT_hi[x.par][:, k, :], xgT_lo[x.par][:, k, :]),
                                     (whi[:, 0:2, F * k:F * (k + 1)], wlo[:, 0:2, F * k:F * (k + 1)]), k == 0, k == KD - 1)
                    return mm

                this = ahead or x.par
                if this:
                    pe.wait_ge(lo_done, 60 + 3 * x.e + 2)
                    pe.wait_ge(xgTl_done, 2 * x.e + 2)
                    gate_up(0, KD // 2)
                if tables:
                    slot_products(x.e + 2, x.e + 3)
                if back:
                    pe.wait_ge(h_done, x.e)
                    for k in range(KF):
                        mm = nc.tensor.transpose(bank[4][:, P * k:P * (k + 1)], ex_h[:].rearrange("p (d k) -> p k d", k=KF)[:, k, :], ident[:])
                    mm.then_inc(exT_ready, 1)
                if ahead:
                    turn_rows(x.next())
                if this:
                    gate_up(KD // 2, KD).then_inc(gu_ready, 1)
                if back:
                    whi, wlo = sets[1 - x.par]
                    pe.wait_ge(exTl_done, x.e)
                    pe.wait_ge(lo_done, 60 + 3 * x.e)
                    pe.wait_ge(y_done, 2 * x.e - 1)
                    for half in range(2):
                        for k in range(KF):
                            mm = product(bank[6 + half][:], (exT_hi[:, k, :], exT_lo[:, k, :]),
                                         (whi[:, 2, D * k + 512 * half:D * k + 512 * (half + 1)],
                                          wlo[:, 2, D * k + 512 * half:D * k + 512 * (half + 1)]), k == 0, k == KF - 1)
                    mm.then_inc(y_ready, 1)

            run_experts(pe, expert_pe, E)

            def over_pe(e, r, n):
                pe.wait_ge(over_hot, n)
                for tt in range(NT):
                    mm = nc.tensor.matmul(bank[5][:, 0:4], one_hot[:, tt, :], route_cols[:, tt, bass.ds(e, 1), :].rearrange("p a c -> p (a c)"),
                                          start=(tt == 0), stop=(tt == NT - 1))
                mm.then_inc(over_lists_ready, 1)
                pe.wait_ge(over_gathered, 16 * n)
                for k in range(KD):
                    mm = nc.tensor.transpose(bank[2 + k // 4][:, P * (k % 4):P * (k % 4 + 1)],
                                             xg[0][:].rearrange("p (d k) -> p k d", k=KD)[:, k, :], ident[:])
                mm.then_inc(over_turned, 1)
                pe.wait_ge(over_lo, 3 * n)
                pe.wait_ge(over_xl, 2 * n)
                for k in range(KD):
                    mm = product(bank[0][:], (xgT_hi[0][:, k, :], xgT_lo[0][:, k, :]),
                                 (split_hi[:, 0:2, F * k:F * (k + 1)], split_lo[:, 0:2, F * k:F * (k + 1)]), k == 0, k == KD - 1)
                mm.then_inc(over_gu, 1)
                pe.wait_ge(over_h, n)
                for k in range(KF):
                    mm = nc.tensor.transpose(bank[4][:, P * k:P * (k + 1)], ex_h[:].rearrange("p (d k) -> p k d", k=KF)[:, k, :], ident[:])
                mm.then_inc(over_exT, 1)
                pe.wait_ge(over_exl, n)
                for half in range(2):
                    for k in range(KF):
                        mm = product(bank[6 + half][:], (exT_hi[:, k, :], exT_lo[:, k, :]),
                                     (split_hi[:, 2, D * k + 512 * half:D * k + 512 * (half + 1)],
                                      split_lo[:, 2, D * k + 512 * half:D * k + 512 * (half + 1)]), k == 0, k == KF - 1)
                mm.then_inc(over_y, 1)

            further_rounds(pe, over_pe)


_INS = ['x', 'p', 'w_in', 'conv_w', 'b_igate', 'b_fgate', 'mlstm_norm_g', 'w_branch_a', 'w_branch_b', 'w_out',
        'ln1_g', 'ln1_b', 'w_router', 'router_bias', 'w_exp_gate', 'w_exp_up', 'w_exp_down', 'w_sh_gate',
        'w_sh_up', 'w_sh_down', 'w_ple_gate', 'w_ple_proj', 'ln2_g', 'ln2_b']


def kernel(**inputs):
    import numpy as _np
    import concourse.bacc as _bacc
    from concourse import mybir as _mybir
    from concourse.bass_utils import run_bass_kernel_spmd as _run

    nc = _bacc.Bacc("TRN2", target_bir_lowering=False, num_devices=1)
    arrays, args = {}, []
    for name in _INS:
        a = _np.ascontiguousarray(inputs[name])
        arrays[f"in_{name}_dram"] = a
        args.append(nc.dram_tensor(f"in_{name}_dram", a.shape, _mybir.dt.from_np(a.dtype), kind="ExternalInput").ap())
    shape = inputs["x"].shape
    args.append(nc.dram_tensor("out_dram", shape, _mybir.dt.float32, kind="ExternalOutput").ap())
    hybrid_layer(nc, *args)
    r = _run(nc, [arrays], core_ids=[0])
    return r.results[0]["out_dram"]
```
